# Optimizing a Trainium2 kernel written in Bass

```python
import jax, jax.numpy as jnp
from jax import lax
import numpy as np

D_MODEL = 1024
BATCH = 1
SEQ = 1024
DEPTH = 2
DEC_BATCH = 1
DEC_SEQ = 64
PAST_LEN = 256

CHUNK = 64
N_MIXERS = 2
N_LRU_LAYERS = (DEPTH + 1) // 2
N_RWKV_LAYERS = DEPTH // 2
LRU_WIDTH = D_MODEL
LRU_BLOCKS = 8
LRU_BLOCK_DIM = LRU_WIDTH // LRU_BLOCKS
LRU_CONV = 4
LRU_C = 8.0
RWKV_HEAD = 64
RWKV_HEADS = D_MODEL // RWKV_HEAD
DECAY_LORA = 64
AAA_LORA = 64
GATE_LORA = 128
D_FF = 3 * D_MODEL
FFN_CONV = 3
RMS_EPS = 1e-6
GN_EPS = 64e-5

kernel_name = 'hybrid_rglru_rwkv7_convffn_stream_step'

def rmsnorm(x, g):
    x32 = x.astype(jnp.float32)
    y = x32 * lax.rsqrt(jnp.mean(x32 * x32, axis=-1, keepdims=True) + RMS_EPS)
    return (y * g.astype(jnp.float32)).astype(x.dtype)

def causal_dwconv(x, buf, w, b):
    k = w.shape[0]
    t = x.shape[1]
    xp = jnp.concatenate([buf.astype(x.dtype), x], axis=1)
    y = b + xp[:, k - 1:k - 1 + t] * w[k - 1]
    for j in range(k - 1):
        y = y + xp[:, j:j + t] * w[j]
    return y, xp[:, t:]

def block_diag(u, w, b):
    bsz, t, _ = u.shape
    ub = u.reshape(bsz, t, LRU_BLOCKS, LRU_BLOCK_DIM)
    return (jnp.einsum('btnc,ncd->btnd', ub, w) + b).reshape(bsz, t, LRU_WIDTH)

def lru_mixer(h, conv_buf, h0, w_x, b_x, w_y, b_y, conv_w, conv_b, ga_w, ga_b, gx_w, gx_b, lam, w_out, b_out):
    gate = jax.nn.gelu(h @ w_y + b_y)
    u, new_buf = causal_dwconv(h @ w_x + b_x, conv_buf, conv_w, conv_b)
    r = jax.nn.sigmoid(block_diag(u, ga_w, ga_b)).astype(jnp.float32)
    i = jax.nn.sigmoid(block_diag(u, gx_w, gx_b))
    log_a = -LRU_C * r * jax.nn.softplus(-lam.astype(jnp.float32))
    a = jnp.exp(log_a)
    bx = jnp.sqrt(-jnp.expm1(2.0 * log_a)) * (i * u).astype(jnp.float32)
    bx = bx.at[:, 0].add(a[:, 0] * h0.astype(jnp.float32))

    def combine(left, right):
        a1, b1 = left
        a2, b2 = right
        return a1 * a2, a2 * b1 + b2

    _, hs = lax.associative_scan(combine, (a, bx), axis=1)
    y = (hs.astype(h.dtype) * gate) @ w_out + b_out
    return y, new_buf, hs[:, -1]

def rwkv7_mixer(h, shift_prev, s0, mu, w_r, w_k, w_v, w_o, w0, w1, w2, a0, a1, a2, g1, g2, k_k, k_a, r_k, ln_w, ln_b):
    bsz, t, c = h.shape
    f32 = jnp.float32
    prev = jnp.concatenate([shift_prev[:, None].astype(h.dtype), h[:, :-1]], axis=1)
    xx = prev - h
    xr, xw, xk, xv, xa, xg = [h + xx * mu[j] for j in range(6)]
    r = xr @ w_r
    k = xk @ w_k
    v = xv @ w_v
    wlog = -jax.nn.softplus(-(w0 + jnp.tanh(xw @ w1) @ w2).astype(f32)) - 0.5
    decay = jnp.exp(-jnp.exp(wlog))
    a = jax.nn.sigmoid(a0 + (xa @ a1) @ a2)
    g = jax.nn.sigmoid(xg @ g1) @ g2
    heads = lambda z: z.astype(f32).reshape(bsz, t, RWKV_HEADS, RWKV_HEAD)
    kk = heads(k * k_k)
    kk = kk / jnp.maximum(jnp.sqrt(jnp.sum(kk * kk, axis=-1, keepdims=True)), 1e-12)
    k = k * (1.0 + (a - 1.0) * k_a)
    r_h, k_h, v_h, w_h, a_h = heads(r), heads(k), heads(v), heads(decay), heads(a)
    tm = lambda z: jnp.swapaxes(z, 0, 1)

    def step(s, inp):
        r_t, w_t, k_t, v_t, aa_t, bb_t = inp
        sa = jnp.einsum('bhij,bhj->bhi', s, aa_t)
        s = s * w_t[:, :, None, :] + sa[..., None] * bb_t[:, :, None, :] + v_t[..., None] * k_t[:, :, None, :]
        return s, jnp.einsum('bhij,bhj->bhi', s, r_t)

    s_last, ys = lax.scan(step, s0.astype(f32),
                          (tm(r_h), tm(w_h), tm(k_h), tm(v_h), tm(-kk), tm(kk * a_h)))
    y = tm(ys)
    mean = jnp.mean(y, axis=-1, keepdims=True)
    var = jnp.mean(jnp.square(y - mean), axis=-1, keepdims=True)
    yn = ((y - mean) * lax.rsqrt(var + GN_EPS)).reshape(bsz, t, c) * ln_w.astype(f32) + ln_b.astype(f32)
    bonus = (jnp.sum(r_h * k_h * r_k.astype(f32), axis=-1, keepdims=True) * v_h).reshape(bsz, t, c)
    out = ((yn + bonus).astype(h.dtype) * g) @ w_o
    return out, h[:, -1], s_last

def conv_ffn(h, buf, w_up, conv_w, conv_b, w_down):
    u, new_buf = causal_dwconv(h @ w_up, buf, conv_w, conv_b)
    g, val = jnp.split(u, 2, axis=-1)
    return (jax.nn.gelu(g) * val) @ w_down, new_buf

def trunk(x, lru_conv, lru_h, rw_shift, rw_wkv, ffn_conv, norm_mix, norm_ffn, norm_final, lru_p, rw_p, ffn_p):
    new_lc, new_lh, new_rs, new_rw, new_fc = [], [], [], [], []
    i_lru = 0
    i_rw = 0
    for layer in range(DEPTH):
        hn = rmsnorm(x, norm_mix[layer])
        if layer % N_MIXERS == 0:
            y, cb, hl = lru_mixer(hn, lru_conv[i_lru], lru_h[i_lru], *[w[i_lru] for w in lru_p])
            new_lc.append(cb)
            new_lh.append(hl)
            i_lru += 1
        else:
            y, sh, sw = rwkv7_mixer(hn, rw_shift[i_rw], rw_wkv[i_rw], *[w[i_rw] for w in rw_p])
            new_rs.append(sh)
            new_rw.append(sw)
            i_rw += 1
        x = x + y
        hn = rmsnorm(x, norm_ffn[layer])
        y, fb = conv_ffn(hn, ffn_conv[layer], *[w[layer] for w in ffn_p])
        new_fc.append(fb)
        x = x + y
    st = lambda lst: jnp.stack(lst).astype(x.dtype)
    return rmsnorm(x, norm_final), st(new_lc), st(new_lh), st(new_rs), st(new_rw), st(new_fc)

def setup_inputs(seed: int = 0) -> dict:
    key = jax.random.key(seed)
    cnt = [0]

    def nk():
        cnt[0] += 1
        return jax.random.fold_in(key, cnt[0])

    nrm = lambda shape, scale: scale * jax.random.normal(nk(), shape, jnp.float32)
    unif = lambda shape, lo, hi: jax.random.uniform(nk(), shape, jnp.float32, lo, hi)
    NA, NB, L = N_LRU_LAYERS, N_RWKV_LAYERS, DEPTH
    D, LW, H, N = D_MODEL, LRU_WIDTH, RWKV_HEADS, RWKV_HEAD
    LB, BD = LRU_BLOCKS, LRU_BLOCK_DIM
    s = unif((NA, LW), 0.9, 0.999) ** (1.0 / LRU_C)
    lam = jnp.log(s) - jnp.log1p(-s)
    return {
        'x_prompt': nrm((BATCH, SEQ, D), 1.0),
        'x_sample': nrm((DEC_BATCH, DEC_SEQ, D), 1.0),
        'state_lru_conv': nrm((NA, DEC_BATCH, LRU_CONV - 1, LW), 1.0),
        'state_lru_h': nrm((NA, DEC_BATCH, LW), 0.5),
        'state_rwkv_shift': nrm((NB, DEC_BATCH, D), 1.0),
        'state_rwkv_wkv': nrm((NB, DEC_BATCH, H, N, N), 0.3),
        'state_ffn_conv': nrm((L, DEC_BATCH, FFN_CONV - 1, 2 * D_FF), 1.0),
        'norm_mix': 1.0 + nrm((L, D), 0.05),
        'norm_ffn': 1.0 + nrm((L, D), 0.05),
        'norm_final': 1.0 + nrm((D,), 0.05),
        'lru_w_x': nrm((NA, D, LW), D ** -0.5),
        'lru_b_x': nrm((NA, LW), 0.02),
        'lru_w_y': nrm((NA, D, LW), D ** -0.5),
        'lru_b_y': nrm((NA, LW), 0.02),
        'lru_conv_w': nrm((NA, LRU_CONV, LW), LRU_CONV ** -0.5),
        'lru_conv_b': nrm((NA, LW), 0.02),
        'lru_ga_w': nrm((NA, LB, BD, BD), BD ** -0.5),
        'lru_ga_b': nrm((NA, LB, BD), 0.02),
        'lru_gx_w': nrm((NA, LB, BD, BD), BD ** -0.5),
        'lru_gx_b': nrm((NA, LB, BD), 0.02),
        'lru_lambda': lam,
        'lru_w_out': nrm((NA, LW, D), LW ** -0.5),
        'lru_b_out': nrm((NA, D), 0.02),
        'rw_mu': unif((NB, 6, D), 0.0, 1.0),
        'rw_w_r': nrm((NB, D, D), D ** -0.5),
        'rw_w_k': nrm((NB, D, D), D ** -0.5),
        'rw_w_v': nrm((NB, D, D), D ** -0.5),
        'rw_w_o': nrm((NB, D, D), D ** -0.5),
        'rw_w0': unif((NB, D), -6.0, -1.0),
        'rw_w1': nrm((NB, D, DECAY_LORA), D ** -0.5),
        'rw_w2': nrm((NB, DECAY_LORA, D), 0.1 * DECAY_LORA ** -0.5),
        'rw_a0': nrm((NB, D), 0.1),
        'rw_a1': nrm((NB, D, AAA_LORA), D ** -0.5),
        'rw_a2': nrm((NB, AAA_LORA, D), 0.1 * AAA_LORA ** -0.5),
        'rw_g1': nrm((NB, D, GATE_LORA), D ** -0.5),
        'rw_g2': nrm((NB, GATE_LORA, D), GATE_LORA ** -0.5),
        'rw_k_k': 0.85 + nrm((NB, D), 0.05),
        'rw_k_a': 1.0 + nrm((NB, D), 0.05),
        'rw_r_k': nrm((NB, H, N), 0.1),
        'rw_ln_w': 1.0 + nrm((NB, D), 0.05),
        'rw_ln_b': nrm((NB, D), 0.02),
        'ffn_w_up': nrm((L, D, 2 * D_FF), D ** -0.5),
        'ffn_conv_w': nrm((L, FFN_CONV, 2 * D_FF), FFN_CONV ** -0.5),
        'ffn_conv_b': nrm((L, 2 * D_FF), 0.02),
        'ffn_w_down': nrm((L, D_FF, D), D_FF ** -0.5),
    }

def reference(x_prompt, x_sample, state_lru_conv, state_lru_h, state_rwkv_shift, state_rwkv_wkv, state_ffn_conv,
              norm_mix, norm_ffn, norm_final,
              lru_w_x, lru_b_x, lru_w_y, lru_b_y, lru_conv_w, lru_conv_b, lru_ga_w, lru_ga_b, lru_gx_w, lru_gx_b,
              lru_lambda, lru_w_out, lru_b_out,
              rw_mu, rw_w_r, rw_w_k, rw_w_v, rw_w_o, rw_w0, rw_w1, rw_w2, rw_a0, rw_a1, rw_a2, rw_g1, rw_g2,
              rw_k_k, rw_k_a, rw_r_k, rw_ln_w, rw_ln_b,
              ffn_w_up, ffn_conv_w, ffn_conv_b, ffn_w_down):
    lru_p = (lru_w_x, lru_b_x, lru_w_y, lru_b_y, lru_conv_w, lru_conv_b, lru_ga_w, lru_ga_b,
             lru_gx_w, lru_gx_b, lru_lambda, lru_w_out, lru_b_out)
    rw_p = (rw_mu, rw_w_r, rw_w_k, rw_w_v, rw_w_o, rw_w0, rw_w1, rw_w2, rw_a0, rw_a1, rw_a2,
            rw_g1, rw_g2, rw_k_k, rw_k_a, rw_r_k, rw_ln_w, rw_ln_b)
    ffn_p = (ffn_w_up, ffn_conv_w, ffn_conv_b, ffn_w_down)
    bp = x_prompt.shape[0]
    z = lambda shape: jnp.zeros(shape, jnp.float32)
    y_prompt, p_lc, p_lh, p_rs, p_rw, p_fc = trunk(
        x_prompt,
        z((N_LRU_LAYERS, bp, LRU_CONV - 1, LRU_WIDTH)), z((N_LRU_LAYERS, bp, LRU_WIDTH)),
        z((N_RWKV_LAYERS, bp, D_MODEL)), z((N_RWKV_LAYERS, bp, RWKV_HEADS, RWKV_HEAD, RWKV_HEAD)),
        z((DEPTH, bp, FFN_CONV - 1, 2 * D_FF)),
        norm_mix, norm_ffn, norm_final, lru_p, rw_p, ffn_p)
    y_sample, s_lc, s_lh, s_rs, s_rw, s_fc = trunk(
        x_sample, state_lru_conv, state_lru_h, state_rwkv_shift, state_rwkv_wkv, state_ffn_conv,
        norm_mix, norm_ffn, norm_final, lru_p, rw_p, ffn_p)
    return (y_prompt, y_sample, p_lc, p_lh, p_rs, p_rw, p_fc, s_lc, s_lh, s_rs, s_rw, s_fc)


_drawn_inputs = setup_inputs


def setup_inputs(seed=0):
    import zlib

    import numpy as np

    out = dict(_drawn_inputs(seed))
    spreads = {}
    factors = {'lru_b_y': 4.114,
     'lru_ga_b': 8.0,
     'lru_gx_b': 7.76,
     'rw_w1': 8.0,
     'rw_w2': 8.0,
     'rw_ln_b': 7.091}
    for name, (base, spread) in spreads.items():
        noise = np.random.default_rng([zlib.crc32(name.encode()), seed]).standard_normal(out[name].shape)
        drawn = base * np.exp(spread * noise) if base else spread * noise
        out[name] = __import__('jax').numpy.asarray(drawn.astype(out[name].dtype))
    for name, factor in factors.items():
        out[name] = (out[name] * factor).astype(out[name].dtype)
    return out
```

```python
from contextlib import ExitStack

import numpy as np

import concourse.bass as bass
from concourse import mybir

ALU = mybir.AluOpType
ACT = mybir.ActivationFunctionType
F32 = mybir.dt.float32
F32R = mybir.dt.float32r

P = 128
D = 1024
KT = D // P
SEQ, DEC = 1024, 64
GAP = 4
SAMPLE = SEQ + GAP
COLS = SAMPLE + DEC
HIST = SAMPLE - 1
CH = 3
CW = COLS // CH
PAD = 4
ROW = PAD + COLS
CHUNK = 64
NCH = (SEQ + DEC) // CHUNK
PACK = NCH * CHUNK
SUMW = PACK // 4
HEADS = 2
FF = 3 * D
FT = FF // P
STEPS = FT // 2
BATCHES = [(0, 6), (6, 12), (12, 17)]
LEVELS = 6
RMS_EPS, GN_EPS = 1e-6, 64e-5
DECAY = float(np.exp(-0.5))
LNS = 20

LRU_GROUPS = KT // 2
N_LRU = 3 * KT
N_FFN = 2 * FT + FT
N_PROJ = 6 + 3 * KT
N_OUT = KT
N_TILES = N_LRU + 2 * N_FFN + N_PROJ + N_OUT

VEC = ["mix0", "mix1", "ffn0", "ffn1", "final", "b_x", "b_y", "cw0", "cw1", "cw2", "cw3", "cb",
       "ga_b", "gx_b", "lam", "b_out", "h0", "lc0", "lc1", "lc2", "shift",
       "mu0", "mu1", "mu2", "mu3", "mu4", "mu5", "w0", "a0"]
VAT = {name: n * KT for n, name in enumerate(VEC)}
NV = len(VEC) * KT
C_ONES, C_BD, C_ID, C_MG, C_ML, C_LV, C_IST, C_SCAN = 0, 128, 256, 384, 512, 576, 960, 1024
C_END = C_SCAN + PACK
PV = ["kk", "ka", "rk", "lnw", "lnb"]
SC = ["decay", "a", "g", "r", "k", "v"]


PRIMED = ("dma_fs1", "dma_m", "dma_state", "k_bonus", "k_out")


class Tally:

    def __init__(self, eng, sems):
        self.eng, self.sems = eng, sems
        self.n, self.latest, self.turn, self.per = {}, None, None, {}

    def at(self, name, n):
        unit = 16 if name.startswith("dma_") else 1
        n += name in PRIMED
        assert n > 0, name
        per = self.per.get(name, 0) if self.turn is not None else 0
        return self.sems[name], self.turn * (unit * per) + unit * n if per else unit * n

    def next(self, name, k=1):
        self.n[name] = self.n.get(name, 0) + k
        return self.at(name, self.n[name])

    def own(self):
        return self.at(self.latest, self.n[self.latest])

    def made(self, name, n=None):
        self.n[name] = self.n.get(name, 0) + 1 if n is None else n
        self.latest = name
        return self.sems[name], 16 if name.startswith("dma_") else 1

    def enter(self, turn, per):
        self.turn, self.per, self.start = turn, per, dict(self.n)

    def leave(self, turns):
        for k, v in self.n.items():
            got = v - self.start.get(k, 0)
            if k in ("taken0", "taken1"):
                self.n[k] += self.per.get(k, 0) * (turns - 1)
                continue
            assert got in (0, self.per.get(k, 0)), (self.eng, k, got)
            if got:
                self.n[k] = self.start.get(k, 0) + got * turns
        self.turn, self.per = None, {}


FFN_TURN = dict(w_lo=12, w_hi=12, dma_w0=6, dma_w1=6, conv=8, hist=8, kept=8, tap=16, gelu=4, p_full=4, p_hi=4,
                p_lo=4, dma_fp0=1, dma_fp1=1, dma_fs0=1, dma_fs1=1, acc_ready=24, taken0=12, taken1=12)
FFN_TURNS = (STEPS - 2) // 2
MIXES = [1, 4, 5, 0, 2, 3]
M_LRU = 1
M_N1 = M_LRU + 4 * KT + LRU_GROUPS * KT
M_FFN1 = M_N1 + 1
M_N2 = M_FFN1 + 2 * FT + STEPS * KT
M_PROJ = M_N2 + 1
M_OUT = M_PROJ + 3 + 6 * KT
M_N3 = M_OUT + KT
M_FFN2 = M_N3 + 1
M_N4 = M_FFN2 + 2 * FT + STEPS * KT
H_FINAL = 9 * KT
W_FFN1 = N_LRU
W_PROJ = W_FFN1 + N_FFN
W_OUT = W_PROJ + N_PROJ
W_FFN2 = W_OUT + N_OUT
NTR = [(0, 4), (4, 8), (8, 12), (12, 16), (16, 17)]
NG = [(c, min(c + 2, NCH)) for c in range(0, NCH, 2)]


def build(nc, io):
    ctx = ExitStack()
    with ctx:
        base = -(-nc.sbuf_base // 64) * 64

        def at(name, shape, offset, dt=F32):
            return nc.alloc_sbuf_tensor_at(name, [P] + shape, dt, offset=base + offset)

        x_at = 0
        h_at = x_at + KT * COLS * 4
        p_at = h_at + 2 * KT * COLS * 4
        t_at = p_at + KT * ROW * 4
        w_at = t_at + 8 * ROW * 4
        c_at = w_at + 24576
        X = at("X", [KT, COLS], x_at)
        HH = at("HH", [KT, COLS], h_at, F32R)
        HL = at("HL", [KT, COLS], h_at + KT * COLS * 4, F32R)
        PH = at("PH", [4, COLS], p_at, F32R)
        PL = at("PL", [4, COLS], p_at + 4 * COLS * 4, F32R)
        HF = at("HF", [KT, ROW], p_at)
        T = at("T", [8, ROW], t_at)
        TR = at("TR", [4, ROW], t_at, F32R)
        RAW = [at(f"RAW{s}", [KT, P], w_at + 4096 * s) for s in range(2)]
        WH = [at(f"WH{s}", [KT, P], w_at + 8192 + 8192 * s, F32R) for s in range(2)]
        WL = [at(f"WL{s}", [KT, P], w_at + 12288 + 8192 * s, F32R) for s in range(2)]
        o = c_at
        CO = at("CO", [C_LV], o); o += C_LV * 4
        V = at("V", [NV], o); o += NV * 4
        DV = at("DV", [14, KT], o); o += 14 * KT * 4
        GW = [at(f"GW{s}", [2, P], o + 1024 * s) for s in range(2)]; o += 2048
        FP = [at(f"FP{s}", [4, 6], o + 96 * s) for s in range(2)]; o += 192
        FS = [at(f"FS{s}", [4, 2, 2], o + 64 * s) for s in range(2)]; o += 128
        ST = at("ST", [KT, 10], o); o += KT * 10 * 4
        PP = at("PP", [4], o); o += 64
        PQ = at("PQ", [4], o); o += 64
        PRIME = at("PRIME", [len(PRIMED), 2], o); o += 64
        assert o + base <= nc.sbuf_usable_end, (o + base, nc.sbuf_usable_end)
        o = h_at
        AR = at("AR", [NCH, 2, HEADS, CHUNK], o); o += NCH * 1024
        G = at("G", [NCH, HEADS, 2 * CHUNK], o); o += NCH * 1024
        ND = at("ND", [NCH, HEADS, CHUNK], o); o += NCH * 512
        LT = at("LT", [NCH, HEADS, CHUNK], o); o += NCH * 512
        UV = at("UV", [NCH, HEADS, CHUNK], o); o += NCH * 512
        BKT = at("BKT", [NCH, P], o); o += NCH * 512
        assert o <= p_at
        o = p_at
        BK = at("BK", [NCH, 2, CHUNK], o); o += NCH * 512
        AS = at("AS", [NCH, CHUNK], o); o += PACK * 4
        MS = at("MS", [NCH, CHUNK], o); o += PACK * 4
        Y = at("Y", [NCH, CHUNK], o); o += PACK * 4
        BON = at("BON", [PACK], o); o += PACK * 4
        Z1 = at("Z1", [PACK], o); o += PACK * 4
        Z2 = at("Z2", [NCH, CHUNK], o); o += PACK * 4
        assert o <= t_at
        o = t_at
        LW = at("LW", [PACK], o); o += PACK * 4
        AA = at("AA", [PACK], o); o += PACK * 4
        GG = at("GG", [PACK], o); o += PACK * 4
        RR = at("RR", [PACK], o); o += PACK * 4
        KK = at("KK", [PACK], o); o += PACK * 4
        X1 = at("X1", [PACK], o); o += PACK * 4
        X2 = at("X2", [PACK], o); o += PACK * 4
        assert o <= w_at
        o = w_at + 8192
        VV = at("VV", [CHUNK + PACK], o); o += (CHUNK + PACK) * 4
        LV = at("LV", [LEVELS, CHUNK], o); o += LEVELS * CHUNK * 4
        IST = at("IST", [CHUNK], o); o += CHUNK * 4
        SCAN = at("SCAN", [PACK], o); o += PACK * 4
        SS = [at(f"SS{s}", [CHUNK], o + 256 * s) for s in range(2)]; o += 512
        SPC = at("SPC", [CHUNK], o); o += 256
        RHS = at("RHS", [CHUNK], o); o += 256
        SIN = at("SIN", [CHUNK], o); o += 256
        assert o <= c_at, (o, c_at)

        PS = ctx.enter_context(nc.psum_tensor("PS", [P, 8, 512], F32))
        ACC = [PS[:, 0:3, 0:CW], PS[:, 3:6, 0:CW]]

        names = """dma_w0 dma_w1 dma_const dma_x dma_gw0 dma_gw1 dma_fp0 dma_fp1 dma_fs0 dma_fs1
            dma_spill0 dma_spill1 dma_in1 dma_in2 dma_gg dma_const2 dma_state dma_m dma_load0 dma_load1
            dma_y0 dma_y1 dma_st
            w_hi w_lo acc_ready taken0 taken1 pads vprep absv hist kept tap conv gelu squared summed rstd
            h_full h_hi h_lo h_used mixhalf hf p_full p_hi p_lo tan root post
            lora lora_hi lora_lo zeroed m_clear
            k_kk k_sq k_sums k_max k_ln k_rn k_elem k_scan k_excl k_exp k_prep k_bonus k_bk k_tr k_bkt k_vt
            k_g k_gm k_lt k_a k_am k_mm k_ms k_mt k_nd k_rhs k_rhss k_sa k_sa0 k_sa1 k_sp k_scale k_s
            k_y k_ys k_cent k_csq k_gln k_grs k_norm k_out""".split()
        sems = {n: ctx.enter_context(nc.semaphore(n)) for n in names}

        def vec(name, k):
            c = VAT[name] + k
            return V[:, c:c + 1]

        ONES, BD, ID = CO[:, 0:P], CO[:, C_BD:C_BD + P], CO[:, C_ID:C_ID + P]
        MG, ML = CO[:, C_MG:C_MG + P], CO[:, C_ML:C_ML + CHUNK]
        HALF = [slice(0, CHUNK), slice(CHUNK, P)]
        scr, scrm = io["scratch"], io["scratch_m"]

        def row3(t):
            return t.rearrange("p (j c) -> p j c", j=CH)

        def sum4():
            return PS[:, 4:8, 0:SUMW]

        def row4(t):
            return t.rearrange("p (j c) -> p j c", j=4)

        def tails(t, keep):
            w = COLS - SEQ
            return t[:, SEQ - w:COLS].rearrange("p (s c) -> p s c", s=2)[:, :, w - keep:w]

        def turned(i, a, b):
            at = 1024 * (i % 2)
            flat = PS[HALF[0], 0:4, :].rearrange("p a b -> p (a b)")[:, at:at + (b - a) * P]
            return flat.rearrange("p (n h c) -> p n h c", h=HEADS, c=CHUNK)

        def chunks(t):
            return t.rearrange("p (n c) -> p n c", c=CHUNK)

        def pick(t, turn, plus=0):
            names = " ".join("abcde"[:len(t.shape) - 2])
            return t[bass.ds(turn + plus, 1)].rearrange(f"o p {names} -> (o p) {names}")

        block = ctx.enter_context(nc.Block())

        @block.sync
        def _(sp):
            t = Tally(sp, sems)

            def weight(n, turn=None):
                s = n % 2
                if n >= 2:
                    sp.wait_ge(*t.at("w_lo", n - 1))
                src = io["weights"][n] if turn is None else pick(io["weights"], turn * 12, n)
                sp.dma_start(RAW[s][:, :, :].rearrange("p k c -> p (k c)"), src).then_inc(*t.made(f"dma_w{s}"))

            for j, name in enumerate(PRIMED[:3]):
                sp.dma_start(PRIME[:, j, :], io["consts"][:, 0:2]).then_inc(sems[name], 16)
            sp.dma_start(V[:, :], io["vectors"]).then_inc(*t.made("dma_const"))
            sp.dma_start(CO[:, :], io["consts"][:, 0:C_LV]).then_inc(*t.made("dma_const"))
            for k in range(KT):
                sp.dma_start(X[:, k, :], io["xT"][k]).then_inc(*t.made("dma_x"))
            weight(0)
            weight(1)
            n = 2
            for g in range(LRU_GROUPS + 1):
                if g < LRU_GROUPS:
                    for f in (2 * g, 2 * g + 1):
                        if f >= 2:
                            sp.wait_ge(*t.at("root", f - 1))
                        sp.dma_start(GW[f % 2][:, :, :], io["gates"][f]).then_inc(*t.made(f"dma_gw{f % 2}"))
                while n < min(N_LRU, 4 + 6 * g) + 2:
                    weight(n)
                    n += 1

            def ffn(layer, first, convs):
                def step(s, tiles, turn=None):
                    b = s % 2
                    if s:
                        sp.wait_ge(*t.at("conv", convs + 4 * (s - 1)))
                    src = io["ffn_vec"][layer, s] if turn is None else pick(io["ffn_vec"][layer], turn * 2, s)
                    sp.dma_start(FP[b][:, :, :], src).then_inc(*t.made(f"dma_fp{b}"))
                    if s >= 1:
                        keep(s - 1, turn)
                    for q in tiles:
                        weight(q, turn)

                def keep(s, turn=None):
                    sp.wait_ge(*t.next("kept", 4))
                    dst = io["ffn_state"][layer, s] if turn is None else pick(io["ffn_state"][layer], turn * 2, s)
                    sp.dma_start(dst, FS[s % 2][:, :, :, :]).then_inc(*t.made(f"dma_fs{s % 2}"))

                t.n["kept"] = convs_kept[layer]
                w = first + 2
                step(0, range(w, w + 4))
                w += 4
                with sp.Fori(0, FFN_TURNS) as turn:
                    t.enter(turn, FFN_TURN)
                    step(1, range(w, w + 6), turn)
                    step(2, range(w + 6, w + 12), turn)
                    t.leave(FFN_TURNS)
                w += 12 * FFN_TURNS
                step(STEPS - 1, range(w, w + 6))
                keep(STEPS - 1)
                for q in range(w + 6, w + 8):
                    if q < N_TILES:
                        weight(q)

            convs_kept = [2 * KT, 2 * KT + 2 * FT]
            ffn(0, W_FFN1, KT)
            for q in range(W_PROJ + 2, W_OUT):
                weight(q)
            sp.wait_ge(*t.at("acc_ready", M_OUT))
            sp.wait_ge(*t.at("h_lo", 8 * 8))
            for p, name in enumerate(("dma_spill0", "dma_spill1")):
                sp.wait_ge(*t.at(name, 24))
            for tile, a, b in ((LV[:, :, :].rearrange("p l c -> p (l c)"), C_LV, C_IST),
                               (IST[:, :], C_IST, C_SCAN), (SCAN[:, :], C_SCAN, C_END)):
                sp.dma_start(tile, io["consts"][:, a:b]).then_inc(*t.made("dma_const2"))
            with sp.Fori(0, KT) as turn:
                t.enter(turn, dict(dma_in1=11, dma_in2=2, dma_gg=2, k_bonus=1, k_out=1, dma_m=1, dma_state=2, k_s=NCH))

                def load(tile, j, event):
                    src = pick(scr[j], turn)
                    sp.dma_start(tile[:, 0:SEQ], src[:, 0:SEQ]).then_inc(*t.made(event))
                    sp.dma_start(tile[:, SEQ:PACK], src[:, SAMPLE:COLS]).then_inc(*t.made(event))
                sp.wait_ge(*t.at("k_bonus", 0))
                load(KK, 4, "dma_in1")
                sp.dma_start(PP[:, :], pick(io["pair_vec"][0], turn)).then_inc(*t.made("dma_in1"))
                load(LW, 0, "dma_in1")
                load(AA, 1, "dma_in1")
                load(RR, 3, "dma_in1")
                sp.wait_ge(*t.at("k_out", 0))
                load(VV[:, CHUNK:], 5, "dma_in1")
                sp.dma_start(SIN[:, :], pick(io["wkv"], turn)).then_inc(*t.made("dma_in2"))
                sp.dma_start(PQ[:, :], pick(io["pair_vec"][1], turn)).then_inc(*t.made("dma_in2"))
                sp.wait_ge(*t.at("dma_m", 0))
                load(GG, 2, "dma_gg")
                for c, k in ((SEQ // CHUNK - 1, SEQ // CHUNK), (NCH - 1, 1)):
                    sp.wait_ge(*t.next("k_s", k))
                    sp.dma_start(pick(io["wkv_out"][c - NCH + 2], turn), SS[c % 2][:, :]).then_inc(*t.made("dma_state"))
                sp.wait_ge(*t.at("k_out", 1))
                sp.dma_start(pick(scrm, turn), GG[:, :]).then_inc(*t.made("dma_m"))
                t.leave(KT)
            sp.wait_ge(*t.at("dma_m", KT))
            weight(W_OUT)
            weight(W_OUT + 1)
            sp.wait_ge(*t.at("m_clear", 1))
            for k in range(KT):
                if k >= 2:
                    sp.wait_ge(*t.at("h_lo", 8 * 8 + k - 1))
                b = k % 2
                sp.dma_start(T[:, 4 + b, 0:SEQ], scrm[k][:, 0:SEQ]).then_inc(*t.made(f"dma_load{b}"))
                sp.dma_start(T[:, 4 + b, SAMPLE:COLS], scrm[k][:, SEQ:PACK]).then_inc(*t.made(f"dma_load{b}"))
            for q in range(W_OUT + 2, W_FFN2 + 2):
                weight(q)
            sp.dma_start(io["small"], ST[:, :, :]).then_inc(*t.made("dma_st"))
            ffn(1, W_FFN2, KT + 2 * FT)
            for k in range(KT):
                sp.wait_ge(*t.at("h_full", H_FINAL + k + 1))
                sp.dma_start(io["yT"][k], T[:, 4 + k % 2, 0:COLS]).then_inc(*t.made(f"dma_y{k % 2}"))
            for name in ("dma_y0", "dma_y1", "dma_st", "dma_fs0", "dma_fs1"):
                sp.wait_ge(*t.at(name, t.n[name]))
            sp.wait_ge(*t.at("dma_state", 2 * KT))

        @block.scalar
        def _(act):
            t = Tally(act, sems)

            def run(out, in_, func, event, bias=0.0, scale=1.0, n=None):
                if t.latest:
                    act.wait_ge(*t.own())
                act.activation(out, in_, func, bias=bias, scale=scale).then_inc(*t.made(event, n))

            def w_hi(n, ready):
                if n >= N_TILES:
                    return
                act.wait_ge(*t.next(f"dma_w{n % 2}"))
                if ready:
                    act.wait_ge(*t.at("acc_ready", ready))
                run(WH[n % 2][:, :, :], RAW[n % 2][:, :, :], ACT.Copy, "w_hi")

            def evacuate(m, out, func, bias=0.0, scale=1.0):
                act.wait_ge(*t.at("acc_ready", m + 1))
                run(out, ACC[m % 2], func, f"taken{m % 2}", bias, scale, m // 2 + 1)

            def norm(m, source, final=False, wkv=False):
                for k in range(KT):
                    source(k)
                    if k >= 3:
                        act.wait_ge(*t.at("summed", t.n.get("squared", 0) // KT * (KT - 1) + k - 2))
                    run(T[:, 3 if k == 0 else 4 + k % 2, 0:COLS], X[:, k, :], ACT.Square, "squared")
                evacuate(m, row3(T[:, 2, 0:COLS]), ACT.Ln, bias=RMS_EPS, scale=1.0 / D)
                run(T[:, 2, 0:COLS], T[:, 2, 0:COLS], ACT.Exp, "rstd", scale=-0.5)

            def h_hi(k, source="h_full"):
                if source:
                    act.wait_ge(*t.next(source))
                run(HH[:, k, :], T[:, 4 + k % 2, 0:COLS], ACT.Copy, "h_hi")

            act.wait_ge(*t.at("dma_const", 2))
            lam = V[:, VAT["lam"]:VAT["lam"] + KT]
            run(DV[:, 6, :], lam, ACT.Abs, "absv")
            run(DV[:, 6, :], DV[:, 6, :], ACT.Exp, "absv", scale=-1.0)
            run(DV[:, 7, :], lam, ACT.Relu, "absv", scale=-1.0)
            w_hi(0, 0)
            w_hi(1, 0)
            act.wait_ge(*t.at("dma_x", KT))
            norm(0, lambda k: None)
            for k in range(KT):
                h_hi(k)

            UB, R, I, S = T[:, 0, PAD:ROW], T[:, 4, 0:COLS], T[:, 5, 0:COLS], T[:, 6, 0:COLS]
            m, n = M_LRU, 2

            def gates(m, f):
                evacuate(m, row3(R), ACT.Sigmoid, bias=vec("ga_b", f))
                evacuate(m + 1, row3(I), ACT.Sigmoid, bias=vec("gx_b", f))
                if f == 0:
                    act.wait_ge(*t.next("vprep"))
                run(R, R, ACT.Tanh, "tan", scale=DV[:, 8, f:f + 1])
                if f:
                    act.wait_ge(*t.at("p_lo", f))
                run(S, R, ACT.Sqrt, "root", scale=4.0)

            def p_hi(slot, src):
                act.wait_ge(*t.next("p_full"))
                run(PH[:, slot, :], src, ACT.Copy, "p_hi")

            for g in range(LRU_GROUPS):
                f = 2 * g
                slot = 2 * (g % 2)
                evacuate(m, row3(T[:, 2, 0:COLS]), ACT.Gelu_apprx_tanh, bias=vec("b_y", f))
                w_hi(n, m + 1)
                evacuate(m + 1, row3(UB), ACT.Identity, bias=vec("b_x", f))
                w_hi(n + 1, m + 2)
                evacuate(m + 2, row3(T[:, 3, 0:COLS]), ACT.Gelu_apprx_tanh, bias=vec("b_y", f + 1))
                w_hi(n + 2, m + 3)
                gates(m + 3, f)
                p_hi(slot, S)
                evacuate(m + 5, row3(UB), ACT.Identity, bias=vec("b_x", f + 1))
                w_hi(n + 3, m + 6)
                m, n = m + 6, n + 4
                if g:
                    w_hi(n, m + 4)
                    w_hi(n + 1, m + 8)
                    m, n = m + KT, n + 2
                gates(m, f + 1)
                p_hi(slot + 1, S)
                m += 2
            w_hi(n, m + 4)
            w_hi(n + 1, m + 8)
            m, n = m + KT, n + 2
            assert (m, n) == (M_N1, W_FFN1 + 2)

            def added(m0):
                return lambda k: act.wait_ge(*t.at(f"taken{(m0 + k) % 2}", (m0 + k) // 2 + 1))

            def ffn(m, n):
                def step(s, m, n):
                    for j in range(2):
                        gate = T[:, 2 + 2 * j, 0:COLS]
                        evacuate(m, row3(T[:, 0, PAD:ROW]), ACT.Copy)
                        w_hi(n, m + 1)
                        act.wait_ge(*t.next("conv"))
                        run(gate, gate, ACT.Gelu_apprx_tanh, "gelu")
                        evacuate(m + 1, row3(T[:, 1, PAD:ROW]), ACT.Copy)
                        w_hi(n + 1, m + 2)
                        act.wait_ge(*t.next("conv"))
                        p_hi(2 * (s % 2) + j, gate)
                        m, n = m + 2, n + 2
                    return m, n

                def down(m, n):
                    w_hi(n, m + 4)
                    w_hi(n + 1, m + 8)
                    return m + KT, n + 2

                m, n = step(0, m, n)
                with act.Fori(0, FFN_TURNS) as turn:
                    if t.latest:
                        act.wait_ge(*t.own())
                    t.enter(turn, FFN_TURN)
                    a, b = m, n
                    for s in (1, 2):
                        a, b = step(s, a, b)
                        a, b = down(a, b)
                    t.leave(FFN_TURNS)
                m, n = m + 24 * FFN_TURNS, n + 12 * FFN_TURNS
                m, n = step(STEPS - 1, m, n)
                m, n = down(m, n)
                return down(m, n)

            norm(m, added(m - KT))
            for k in range(KT):
                h_hi(k)
            act.wait_ge(*t.next("conv", KT))
            m, n = ffn(M_FFN1, n)
            assert (m, n) == (M_N2, W_PROJ + 2)
            norm(m, added(m - KT))

            m = M_PROJ

            def mix_hi(m, k):
                if k < KT - 1:
                    act.wait_ge(*t.next("h_used"))
                else:
                    act.wait_ge(*t.at("acc_ready", m + 1))
                h_hi(k)

            for k in range(KT):
                h_hi(k)
            for k in range(KT):
                mix_hi(m, k)
            lora, lora_g = T[:, 6, 0:COLS], T[:, 7, 0:COLS]
            half_acc = lambda m, h: ACC[m % 2][HALF[h]]
            act.wait_ge(*t.at("acc_ready", m + 1))
            run(row3(lora)[HALF[0]], half_acc(m, 0), ACT.Tanh, f"taken{m % 2}", n=m // 2 + 1)
            w_hi(n, m + 1)
            for k in range(KT):
                mix_hi(m + 1, k)
            act.wait_ge(*t.at("acc_ready", m + 2))
            run(row3(lora)[HALF[1]], half_acc(m + 1, 1), ACT.Copy, f"taken{(m + 1) % 2}", n=(m + 1) // 2 + 1)
            w_hi(n + 1, m + 2)
            run(TR[:, 0, 0:COLS], lora, ACT.Copy, "lora_hi")
            evacuate(m + 2, row3(lora_g), ACT.Sigmoid)
            w_hi(n + 2, m + 3)
            run(TR[:, 2, 0:COLS], lora_g, ACT.Copy, "lora_hi")
            act.wait_ge(*t.at("lora_lo", 2))
            m0, m, n = m, m + 3, n + 3
            spills = 0

            def spill(m, j, f, func, bias=0.0):
                nonlocal spills
                b = spills % 2
                if spills >= 2:
                    act.wait_ge(*t.at(f"dma_spill{b}", spills // 2))
                evacuate(m, row3(T[:, 6 + b, 0:COLS]), func, bias=bias)
                if t.latest:
                    act.wait_ge(*t.own())
                act.dma_start(scr[j, f], T[:, 6 + b, 0:COLS]).then_inc(*t.made(f"dma_spill{b}"))
                t.latest = f"taken{m % 2}"
                spills += 1

            for j in range(3):
                for f in range(KT):
                    if j == 0:
                        spill(m, j, f, ACT.Sigmoid, vec("w0", f))
                        mix_hi(m0 + 2, f)
                    elif j == 1:
                        spill(m, j, f, ACT.Sigmoid, vec("a0", f))
                    else:
                        spill(m, j, f, ACT.Copy)
                    m += 1
                w_hi(n, m)
                n += 1
            for j in range(3, 6):
                for f in range(KT):
                    if f == KT - 1 and j < 5:
                        for k in range(KT):
                            mix_hi(m, k)
                    spill(m, j, f, ACT.Copy)
                    m += 1
                    if j < 5 or f < KT - 2:
                        w_hi(n, m)
                        n += 1
            assert m == M_OUT

            act.wait_ge(*t.at("dma_spill0", 24))
            act.wait_ge(*t.at("dma_spill1", 24))
            with act.Fori(0, KT) as turn:
                if t.latest:
                    act.wait_ge(*t.own())
                t.enter(turn, HEAD)
                t.latest = None
                act.wait_ge(*t.at("k_out", 0))
                act.wait_ge(*t.next("dma_in1", 11))
                run(X1[:, :], KK[:, :], ACT.Copy, "k_kk", scale=PP[:, 0:1])
                run(X2[:, :], X1[:, :], ACT.Square, "k_sq")
                act.wait_ge(*t.next("k_scan"))
                run(Z2[:, :, :].rearrange("p n c -> p (n c)"), Z1[:, :], ACT.Exp, "k_exp", scale=-DECAY)
                act.wait_ge(*t.next("k_excl"))
                run(LW[:, :], LW[:, :], ACT.Exp, "k_exp", scale=-DECAY)
                run(Z1[:, :], Z1[:, :], ACT.Exp, "k_exp", scale=DECAY)
                act.wait_ge(*t.next("k_max"))
                run(X2[:, :], X2[:, :], ACT.Ln, "k_ln", scale=float(2 ** LNS))
                run(X2[:, :], X2[:, :], ACT.Exp, "k_rn", scale=-0.5, bias=0.5 * LNS * float(np.log(2.0)))
                for i, (a, b) in enumerate(NTR):
                    act.wait_ge(*t.at("k_tr", 2 * i + 1))
                    run(BKT[:, a:b, :], PS[:, 0, 0:(b - a) * P].rearrange("p (n c) -> p n c", c=P), ACT.Copy, "k_bkt")
                for level in range(LEVELS):
                    for i, (a, b) in enumerate(BATCHES):
                        act.wait_ge(*t.next("k_mt"))
                        for h in range(HEADS):
                            run(ND[HALF[h], a:b, h, :], turned(i, a, b)[:, :, h, :], ACT.Copy, "k_nd")
                for c in range(NCH):
                    act.wait_ge(*t.next("k_rhs"))
                    run(RHS[:, :], PS[:, 2, 0:CHUNK], ACT.Copy, "k_rhss")
                    act.wait_ge(*t.next("k_sa"))
                    run(UV[HALF[0], c, 1, :], PS[HALF[1], 3, 0:CHUNK], ACT.Copy, "k_sa1")
                    act.wait_ge(*t.next("k_y"))
                    run(Y[:, c, :], PS[:, 5, 0:CHUNK], ACT.Copy, "k_ys")
                act.wait_ge(*t.next("k_cent"))
                run(X2[:, :], X1[:, :], ACT.Square, "k_csq")
                act.wait_ge(*t.at("k_sums", 16))
                run(row4(X2[:, :]), sum4(), ACT.Ln, "k_gln", scale=1.0 / CHUNK, bias=GN_EPS)
                run(X2[:, :], X2[:, :], ACT.Exp, "k_grs", scale=-0.5)
                t.leave(KT)
            act.wait_ge(*t.at("k_out", KT))
            act.wait_ge(*t.at("dma_state", 2 * KT))
            w_hi(W_OUT, M_OUT)
            w_hi(W_OUT + 1, M_OUT)
            for k in range(KT):
                act.wait_ge(*t.next(f"dma_load{k % 2}", 2))
                h_hi(k, None)
            m, n = M_OUT, W_OUT + 2
            for f in range(KT):
                w_hi(n, m + 1)
                m, n = m + 1, n + 1
            norm(m, added(m - KT))
            for k in range(KT):
                h_hi(k)
            m, n = ffn(M_FFN2, n)
            assert m == M_N4
            norm(m, added(m - KT))

        @block.gpsimd
        def _(pool):
            t = Tally(pool, sems)

            def rest(out, full, hi, wait, event):
                pool.wait_ge(*t.next(wait))
                if t.latest:
                    pool.wait_ge(*t.own())
                pool.tensor_tensor(out, full, hi, ALU.subtract).then_inc(*t.made(event))

            n = 0

            def w_lo(k=1):
                nonlocal n
                for _ in range(k):
                    if n < N_TILES:
                        s = n % 2
                        rest(WL[s][:, :, :], RAW[s][:, :, :], WH[s][:, :, :], "w_hi", "w_lo")
                        n += 1

            def h_lo(k):
                rest(HL[:, k, :], T[:, 4 + k % 2, 0:COLS], HH[:, k, :], "h_hi", "h_lo")

            def p_lo(slot, full):
                rest(PL[:, slot, :], full, PH[:, slot, :], "p_hi", "p_lo")

            w_lo(2)
            for k in range(KT):
                h_lo(k)
            S = T[:, 6, 0:COLS]
            for g in range(LRU_GROUPS):
                slot = 2 * (g % 2)
                w_lo(3)
                p_lo(slot, S)
                w_lo(1)
                if g:
                    w_lo(2)
                p_lo(slot + 1, S)
            w_lo(2)

            def ffn():
                nonlocal n

                def step(s):
                    for j in range(2):
                        w_lo(2)
                        p_lo(2 * (s % 2) + j, T[:, 2 + 2 * j, 0:COLS])

                step(0)
                with pool.Fori(0, FFN_TURNS) as turn:
                    if t.latest:
                        pool.wait_ge(*t.own())
                    t.enter(turn, FFN_TURN)
                    for s in (1, 2):
                        step(s)
                        w_lo(2)
                    t.leave(FFN_TURNS)
                n += 12 * (FFN_TURNS - 1)
                step(STEPS - 1)
                w_lo(2)
                w_lo(2)

            for k in range(KT):
                h_lo(k)
            ffn()
            assert n == W_PROJ + 2
            for k in range(2 * KT):
                h_lo(k % KT)
            w_lo()
            for k in range(KT):
                h_lo(k)
            w_lo()
            rest(TR[:, 1, 0:COLS], T[:, 6, 0:COLS], TR[:, 0, 0:COLS], "lora_hi", "lora_lo")
            w_lo()
            rest(TR[:, 3, 0:COLS], T[:, 7, 0:COLS], TR[:, 2, 0:COLS], "lora_hi", "lora_lo")
            for k in range(KT):
                h_lo(k)
            w_lo(3)
            for j in range(3):
                for f in range(KT):
                    if f == KT - 1 and j < 2:
                        for k in range(KT):
                            h_lo(k)
                    if j < 2 or f < KT - 2:
                        w_lo()
            assert n == W_OUT
            pool.wait_ge(*t.at("acc_ready", M_OUT))
            for z in (AR[:, :, :, :, :], ND[:, :, :, :], LT[:, :, :, :], UV[:, :, :, :], VV[:, 0:CHUNK]):
                if t.latest:
                    pool.wait_ge(*t.own())
                pool.memset(z, 0.0).then_inc(*t.made("zeroed"))
            w_lo(2)
            for k in range(KT):
                h_lo(k)
            w_lo(KT)
            for k in range(KT):
                h_lo(k)
            ffn()

        @block.tensor
        def _(pe):
            t = Tally(pe, sems)

            def split_product(m, blocks, last=None):
                acc = ACC[m % 2]
                if m >= 2:
                    pe.wait_ge(*t.at(f"taken{m % 2}", m // 2))
                for i, (wh, wl, xh, xl, before, after) in enumerate(blocks):
                    if before:
                        before()
                    for q, (a, b) in enumerate(((wh, xh), (wh, xl), (wl, xh))):
                        for j in range(CH):
                            mm = pe.matmul(acc[:, j, :], a, b[:, j * CW:(j + 1) * CW],
                                           start=(i == 0 and q == 0), stop=(i == len(blocks) - 1 and q == 2))
                    if after:
                        mm.then_inc(*t.made(after))
                mm.then_inc(*t.made("acc_ready"))

            def up(m, n, fresh=False, release=False):
                s = n % 2
                pe.wait_ge(*t.next("w_lo"))
                split_product(m, [(WH[s][:, k, :], WL[s][:, k, :], HH[:, k, :], HL[:, k, :],
                                   (lambda: pe.wait_ge(*t.next("h_lo"))) if fresh else None,
                                   "h_used" if release and k < KT - 1 else None) for k in range(KT)])

            def down(m, n, s):
                pe.wait_ge(*t.next("p_lo", 2))
                for d in range(KT):
                    if d % 4 == 0:
                        pe.wait_ge(*t.next("w_lo"))
                    w = (n + d // 4) % 2
                    split_product(m + d, [(WH[w][:, 2 * (d % 4) + k, :], WL[w][:, 2 * (d % 4) + k, :],
                                           PH[:, 2 * (s % 2) + k, :], PL[:, 2 * (s % 2) + k, :], None, None)
                                          for k in range(2)])
                return m + KT, n + 2

            def norm(m):
                pe.wait_ge(*t.next("summed", KT - 1))
                if m >= 2:
                    pe.wait_ge(*t.at(f"taken{m % 2}", m // 2))
                for j in range(CH):
                    mm = pe.matmul(ACC[m % 2][:, j, :], ONES, T[:, 3, j * CW:(j + 1) * CW], start=True, stop=True)
                mm.then_inc(*t.made("acc_ready"))

            pe.wait_ge(*t.at("dma_const", 2))
            norm(0)
            m, n = M_LRU, 0

            def gates(m, f):
                pe.wait_ge(*t.next("conv"))
                pe.wait_ge(*t.next(f"dma_gw{f % 2}"))
                for q in range(2):
                    if m + q >= 2:
                        pe.wait_ge(*t.at(f"taken{(m + q) % 2}", (m + q) // 2))
                    for j in range(CH):
                        mm = pe.matmul(ACC[(m + q) % 2][:, j, :], GW[f % 2][:, q, :], T[:, 1, j * CW:(j + 1) * CW],
                                       start=True, stop=True)
                    mm.then_inc(*t.made("acc_ready"))

            for g in range(LRU_GROUPS):
                for q in range(3):
                    up(m + q, n + q, fresh=(g == 0 and q == 0))
                gates(m + 3, 2 * g)
                up(m + 5, n + 3)
                m, n = m + 6, n + 4
                if g:
                    m, n = down(m, n, g - 1)
                gates(m, 2 * g + 1)
                m += 2
            m, n = down(m, n, LRU_GROUPS - 1)
            norm(m)
            m += 1

            def ffn(m, n):
                def step(m, n, fresh=False):
                    for q in range(4):
                        up(m + q, n + q, fresh=fresh and q == 0)
                    return m + 4, n + 4

                m, n = step(m, n, fresh=True)
                with pe.Fori(0, FFN_TURNS) as turn:
                    t.enter(turn, FFN_TURN)
                    a, b = m, n
                    for s in (1, 2):
                        a, b = step(a, b)
                        a, b = down(a, b, s - 1)
                    t.leave(FFN_TURNS)
                m, n = m + 24 * FFN_TURNS, n + 12 * FFN_TURNS
                m, n = step(m, n)
                m, n = down(m, n, STEPS - 2)
                return down(m, n, STEPS - 1)

            m, n = ffn(m, n)
            norm(m)
            m += 1
            for q in range(3):
                up(m + q, n + q, fresh=True, release=True)
            m, n = m + 3, n + 3
            for j in range(3):
                pe.wait_ge(*t.next("w_lo"))
                pe.wait_ge(*t.at("lora_lo", 2 if j == 2 else 1))
                s, r = n % 2, 2 if j == 2 else 0
                for f in range(KT):
                    split_product(m, [(WH[s][:, f, :], WL[s][:, f, :], TR[:, r, 0:COLS], TR[:, r + 1, 0:COLS], None, None)])
                    m += 1
                n += 1
            with pe.Fori(0, 3) as turn:
                t.enter(turn, dict(w_lo=KT, h_lo=KT, acc_ready=KT, taken0=KT // 2, taken1=KT // 2, h_used=KT - 1))
                for f in range(KT):
                    up(m + f, n + f, fresh=(f == 0), release=(f == KT - 1))
                t.leave(3)
            m, n = m + 3 * KT, n + 3 * KT
            assert (m, n) == (M_OUT, W_OUT)

            def sums(src):
                for j in range(4):
                    pe.matmul(PS[:, 4 + j, 0:SUMW], BD, src[:, j * SUMW:(j + 1) * SUMW],
                              start=True, stop=True).then_inc(*t.made("k_sums"))

            pe.wait_ge(*t.at("zeroed", 5))
            pe.wait_ge(*t.at("dma_const2", 3))
            pe.wait_ge(*t.at("taken0", (M_OUT + 1) // 2))
            pe.wait_ge(*t.at("taken1", M_OUT // 2))
            with pe.Fori(0, KT) as turn:
                t.enter(turn, HEAD)
                pe.wait_ge(*t.next("k_sq"))
                sums(X2)
                pe.wait_ge(*t.next("k_prep"))
                pe.wait_ge(*t.next("k_max"))
                sums(AA)
                pe.wait_ge(*t.next("k_bk"))
                for i, (a, b) in enumerate(NTR):
                    if i:
                        pe.wait_ge(*t.at("k_bkt", i))
                    for c in range(a, b):
                        mm = pe.transpose(PS[:, 0, (c - a) * P:(c - a + 1) * P],
                                          BK[:, c, :, :].rearrange("p s c -> p (s c)"), ID)
                    mm.then_inc(*t.made("k_tr"))
                    if i:
                        pe.wait_ge(*t.at("k_vt", i))
                    for c in range(a, b):
                        mm = pe.transpose(PS[:, 1, (c - a) * P:(c - a + 1) * P], VV[:, c * CHUNK:(c + 2) * CHUNK], ID)
                    mm.then_inc(*t.made("k_tr"))
                for i, (a, b) in enumerate(NG):
                    if i == 0:
                        pe.wait_ge(*t.at("k_bkt", len(NTR)))
                    elif i == 1:
                        pe.wait_ge(*t.at("k_vt", len(NTR)))
                    else:
                        pe.wait_ge(*t.at("k_gm", i - 1))
                    for c in range(a, b):
                        for h in range(HEADS):
                            col = ((c - a) * HEADS + h) * P
                            mm = pe.matmul(PS[:, i % 2, col:col + P].rearrange("p (s c) -> p s c", s=2),
                                           BK[:, c, :, :].rearrange("p s c -> p (s c)"), AR[:, c, :, h, :],
                                           start=True, stop=True)
                    mm.then_inc(*t.made("k_g"))
                for level in range(LEVELS):
                    for i, (a, b) in enumerate(BATCHES):
                        if level:
                            pe.wait_ge(*t.at("k_ms", 3 * (level - 1) + i + 1))
                        elif i == 0:
                            pe.wait_ge(*t.next("k_lt", 2 * len(NG)))
                            pe.wait_ge(*t.next("k_bonus"))
                        for c in range(a, b):
                            mm = pe.matmul(PS[:, 4 + i, (c - a) * CHUNK:(c - a + 1) * CHUNK],
                                           LT[:, c, :, :].rearrange("p h c -> p (h c)"),
                                           MS[:, c, :] if level else IST[:, :], start=True, stop=True)
                        mm.then_inc(*t.made("k_a"))
                    for i, (a, b) in enumerate(BATCHES if level else []):
                        pe.wait_ge(*t.at("k_am", 3 * level + i + 1))
                        pe.wait_ge(*t.at("k_nd", 6 * (level - 1) + 2 * i + 2))
                        for c in range(a, b):
                            mm = pe.matmul(PS[:, 4 + i, (c - a) * CHUNK:(c - a + 1) * CHUNK],
                                           ND[:, c, :, :].rearrange("p h c -> p (h c)"), AS[:, c, :], start=True, stop=True)
                        mm.then_inc(*t.made("k_mm"))
                    for i, (a, b) in enumerate(BATCHES):
                        pe.wait_ge(*t.at("k_ms", 3 * level + i + 1))
                        if level == 0 and i == 0:
                            pe.wait_ge(*t.at("k_gm", len(NG)))
                        if level or i == 2:
                            pe.wait_ge(*t.at("k_nd", 6 * level + 2 * (i - 1) if i == 2 else 6 * level))
                        at = 1024 * (i % 2)
                        for c in range(a, b):
                            bank, col = divmod(at + (c - a) * P, 512)
                            mm = pe.matmul(PS[HALF[0], bank, col:col + P], MS[:, c, :], ID, start=True, stop=True)
                        mm.then_inc(*t.made("k_mt"))
                pe.wait_ge(*t.at("k_nd", 6 * LEVELS))
                for c in range(NCH):
                    first = c == 0
                    S = SIN if c == NCH - 1 else SS[(c - 1) % 2]
                    for h in range(HEADS):
                        mm = pe.matmul(PS[HALF[h], 2, 0:CHUNK], G[:, c, h, 0:CHUNK], UV[:, c, h, :],
                                       start=True, stop=first, skip_group_check=True)
                    if not first:
                        if c < NCH - 1:
                            pe.wait_ge(*t.at("k_s", c))
                        else:
                            pe.wait_ge(*t.next("dma_in2", 2))
                        mm = pe.matmul(PS[:, 2, 0:CHUNK], AR[:, c, 0, :, :].rearrange("p h c -> p (h c)"), S[:, :],
                                       start=False, stop=True, skip_group_check=True)
                    mm.then_inc(*t.made("k_rhs"))
                    pe.wait_ge(*t.next("k_rhss"))
                    pe.matmul(PS[:, 3, 0:CHUNK], ND[:, c, :, :].rearrange("p h c -> p (h c)"), RHS[:, :],
                              start=True, stop=True, skip_group_check=True).then_inc(*t.made("k_sa"))
                    pe.wait_ge(*t.next("k_sa0"))
                    pe.wait_ge(*t.next("k_sa1"))
                    for h in range(HEADS):
                        mm = pe.matmul(PS[HALF[h], 4, 0:CHUNK], BKT[:, c, h * CHUNK:(h + 1) * CHUNK],
                                       UV[:, c, h, :], start=True, stop=True, skip_group_check=True)
                    mm.then_inc(*t.made("k_sp"))
                    if not first:
                        pe.wait_ge(*t.at("k_ys", c))
                    for h in range(HEADS):
                        out = PS[HALF[h], 5, 0:CHUNK]
                        if not first:
                            pe.matmul(out, S[:, :], AR[:, c, 1, h, :], start=True, stop=False, skip_group_check=True)
                        mm = pe.matmul(out, UV[:, c, h, :], G[:, c, h, CHUNK:2 * CHUNK], start=first, stop=True,
                                       skip_group_check=True)
                    mm.then_inc(*t.made("k_y"))
                pe.wait_ge(*t.at("k_ys", NCH))
                pe.wait_ge(*t.at("k_s", NCH))
                sums(Y[:, :, :].rearrange("p n c -> p (n c)"))
                pe.wait_ge(*t.next("k_csq"))
                sums(X2)
                t.leave(KT)
            pe.wait_ge(*t.at("k_gln", KT))
            for f in range(KT):
                up(m, n, fresh=(f == 0))
                m, n = m + 1, n + 1
            norm(m)
            m += 1
            m, n = ffn(m, n)
            norm(m)
            assert (m, n) == (M_N4, N_TILES)

        @block.vector
        def _(dve):
            t = Tally(dve, sems)

            def tt(out, a, b, op, event, n=None):
                if t.latest:
                    dve.wait_ge(*t.own())
                dve.tensor_tensor(out, a, b, op).then_inc(*t.made(event, n))

            def ts(out, a, s1, s2, op1, op2, event):
                if t.latest:
                    dve.wait_ge(*t.own())
                dve.tensor_scalar(out, a, s1, s2, op1, op2).then_inc(*t.made(event))

            def stt(out, a, s, b, op1, op2, event, n=None):
                if t.latest:
                    dve.wait_ge(*t.own())
                dve.scalar_tensor_tensor(out=out, in0=a, scalar=s, in1=b, op0=op1, op1=op2).then_inc(*t.made(event, n))

            def copy(out, a, event):
                if t.latest:
                    dve.wait_ge(*t.own())
                dve.tensor_copy(out, a).then_inc(*t.made(event))

            def fill(out, value, event):
                if t.latest:
                    dve.wait_ge(*t.own())
                dve.memset(out, value).then_inc(*t.made(event))

            def norm_sums():
                dve.wait_ge(*t.next("squared"))
                for k in range(1, KT):
                    dve.wait_ge(*t.next("squared"))
                    tt(T[:, 3, 0:COLS], T[:, 3, 0:COLS], T[:, 4 + k % 2, 0:COLS], ALU.add, "summed")

            def h_rows(name, at, event="h_full"):
                dve.wait_ge(*t.next("rstd"))
                for k in range(KT):
                    if event == "hf":
                        out = HF[:, k, PAD:ROW]
                    else:
                        out = T[:, 4 + k % 2, 0:COLS]
                        if name == "final":
                            if k >= 2:
                                dve.wait_ge(*t.at(f"dma_y{k % 2}", k // 2))
                        elif k >= 2:
                            dve.wait_ge(*t.at("h_lo", at + k - 1))
                    stt(out, X[:, k, :], vec(name, k), T[:, 2, 0:COLS], ALU.mult, ALU.mult, event)

            def conv(src, out, taps, bias):
                last = len(taps) - 1
                ts(out, src[:, PAD:ROW], taps[last], bias, ALU.mult, ALU.add, "tap")
                for j in range(last - 1, -1, -1):
                    back = last - j
                    stt(out, src[:, PAD - back:ROW - back], taps[j], out, ALU.mult, ALU.add, "tap" if j else "conv")

            def take(m, d, bias=None):
                dve.wait_ge(*t.at("acc_ready", m + 1))
                x = row3(X[:, d, :])
                if bias is None:
                    tt(x, ACC[m % 2], x, ALU.add, f"taken{m % 2}", m // 2 + 1)
                else:
                    stt(x, ACC[m % 2], bias, x, ALU.add, ALU.add, f"taken{m % 2}", m // 2 + 1)

            def take_all(m, last, bias=False):
                for d in range(KT):
                    take(m + d, d, vec("b_out", d) if bias else None)
                if last:
                    norm_sums()

            for j in range(3, len(PRIMED)):
                dve.memset(PRIME[:, j, :], 0.0).then_inc(sems[PRIMED[j]], 1)
            dve.wait_ge(*t.at("dma_const", 2))
            fill(T[:, 0:2, 0:PAD], 0.0, "pads")
            ts(DV[:, 0:6, :].rearrange("p a b -> p (a b)"), V[:, VAT["mu0"]:VAT["mu0"] + 6 * KT], -1.0, 1.0, ALU.mult, ALU.add, "pads")
            dve.wait_ge(*t.next("absv", 3))
            E_, Z_, W_, A_ = DV[:, 6, :], DV[:, 9, :], DV[:, 10, :], DV[:, 11, :]
            ts(Z_, E_, 2.0, None, ALU.add, ALU.bypass, "pads")
            if t.latest:
                dve.wait_ge(*t.own())
            dve.reciprocal(Z_, Z_).then_inc(*t.made("pads"))
            tt(Z_, Z_, E_, ALU.mult, "pads")
            tt(W_, Z_, Z_, ALU.mult, "pads")
            ts(A_, W_, 1.0 / 15, None, ALU.mult, ALU.bypass, "pads")
            for c in (13, 11, 9, 7, 5, 3):
                stt(A_, A_, 1.0 / c, W_, ALU.add, ALU.mult, "pads")
            stt(A_, A_, 1.0, Z_, ALU.add, ALU.mult, "pads")
            stt(DV[:, 8, :], A_, 2.0, DV[:, 7, :], ALU.mult, ALU.add, "pads")
            ts(DV[:, 8, :], DV[:, 8, :], 4.0, None, ALU.mult, ALU.bypass, "vprep")
            norm_sums()
            h_rows("mix0", 0)

            UB, U = T[:, 0, :], T[:, 1, 0:COLS]
            R, I, S, Q = (T[:, r, 0:COLS] for r in (4, 5, 6, 7))

            def lru_conv(m, f):
                dve.wait_ge(*t.at(f"taken{m % 2}", m // 2 + 1))
                for j in range(3):
                    copy(UB[:, PAD + HIST - 2 + j:PAD + HIST - 1 + j], vec(f"lc{j}", f), "hist")
                copy(ST[:, f, 0:6].rearrange("p (s c) -> p s c", s=2), tails(UB[:, PAD:], 3), "kept")
                conv(UB, U, [vec(f"cw{j}", f) for j in range(4)], vec("cb", f))

            def lru_scan(m, f):
                dve.wait_ge(*t.at(f"taken{(m + 1) % 2}", (m + 1) // 2 + 1))
                tt(I, I, U, ALU.mult, "post")
                dve.wait_ge(*t.next("tan"))
                ts(Q, R, 1.0, None, ALU.add, ALU.bypass, "post")
                if t.latest:
                    dve.wait_ge(*t.own())
                dve.reciprocal(Q, Q).then_inc(*t.made("post"))
                dve.wait_ge(*t.next("root"))
                ts(R, Q, 2.0, -1.0, ALU.mult, ALU.add, "post")
                tt(S, S, Q, ALU.mult, "post")
                tt(S, S, I, ALU.mult, "post")
                fill(R[:, HIST:SAMPLE], 0.0, "post")
                copy(S[:, HIST:SAMPLE], vec("h0", f), "post")
                if t.latest:
                    dve.wait_ge(*t.own())
                dve.tensor_tensor_scan(Q, R, S, 0.0, ALU.mult, ALU.add).then_inc(*t.made("post"))
                copy(ST[:, f, 6:8].rearrange("p (s c) -> p s c", s=2), tails(Q, 1), "kept")
                tt(S, Q, T[:, 2 + f % 2, 0:COLS], ALU.mult, "p_full")

            m = M_LRU
            for g in range(LRU_GROUPS):
                f = 2 * g
                lru_conv(m + 1, f)
                lru_scan(m + 3, f)
                lru_conv(m + 5, f + 1)
                m += 6
                if g:
                    take_all(m, False, bias=(g == 1))
                    m += KT
                lru_scan(m, f + 1)
                m += 2
            take_all(m, True)
            m += KT
            fill(T[:, 0:2, 0:PAD], 0.0, "pads")
            h_rows("ffn0", KT)
            m += 1

            def ffn(m, stored):
                def step(s, m):
                    b = s % 2
                    dve.wait_ge(*t.next(f"dma_fp{b}"))
                    if s or stored:
                        dve.wait_ge(*t.at(f"dma_fs{b}", stored + s // 2))
                    for j in range(2):
                        gate, val = T[:, 2 + 2 * j, 0:COLS], T[:, 3 + 2 * j, 0:COLS]
                        dve.wait_ge(*t.at("p_lo", t.n.get("p_full", 0) - 1))
                        for q, out in ((0, gate), (1, val)):
                            v = FP[b][:, 2 * j + q, :]
                            ub = T[:, q, :]
                            dve.wait_ge(*t.at(f"taken{m % 2}", m // 2 + 1))
                            copy(ub[:, PAD + HIST - 1:PAD + SAMPLE], v[:, 4:6], "hist")
                            copy(FS[b][:, 2 * j + q, :, :], tails(ub[:, PAD:], 2), "kept")
                            conv(ub, out, [v[:, c:c + 1] for c in range(3)], v[:, 3:4])
                            m += 1
                        dve.wait_ge(*t.next("gelu"))
                        tt(gate, gate, val, ALU.mult, "p_full")
                    return m

                m = step(0, m)
                with dve.Fori(0, FFN_TURNS) as turn:
                    if t.latest:
                        dve.wait_ge(*t.own())
                    t.enter(turn, FFN_TURN)
                    a = m
                    for s in (1, 2):
                        a = step(s, a)
                        take_all(a, False)
                        a += KT
                    t.leave(FFN_TURNS)
                m += 24 * FFN_TURNS
                m = step(STEPS - 1, m)
                take_all(m, False)
                m += KT
                take_all(m, True)
                return m + KT

            m = ffn(m, 0)
            h_rows("mix1", 0, "hf")
            fill(HF[:, :, PAD - 1:PAD], 0.0, "hf")
            copy(HF[:, :, PAD + HIST:PAD + SAMPLE], V[:, VAT["shift"]:VAT["shift"] + KT].rearrange("p (k c) -> p k c", c=1), "hf")
            w = COLS - SEQ
            copy(ST[:, :, 8:10], HF[:, :, PAD + SEQ - w:ROW].rearrange("p k (s c) -> p k s c", s=2)[:, :, :, w - 1], "hf")
            q = 2 * KT
            for j in MIXES:
                for k in range(KT):
                    tmp = T[:, 4 + k % 2, 0:COLS]
                    dve.wait_ge(*t.at("h_lo", q - 1))
                    ts(tmp, HF[:, k, PAD:ROW], DV[:, j, k:k + 1], None, ALU.mult, ALU.bypass, "mixhalf")
                    stt(tmp, HF[:, k, PAD - 1:ROW - 1], vec(f"mu{j}", k), tmp, ALU.mult, ALU.add, "h_full")
                    q += 1

            dve.wait_ge(*t.at("zeroed", 5))
            dve.wait_ge(*t.at("dma_const2", 3))
            flat = lambda z: z.rearrange("p n c -> p (n c)")
            with dve.Fori(0, KT) as turn:
                if t.latest:
                    dve.wait_ge(*t.own())
                t.enter(turn, HEAD)
                t.latest, t.n["k_out"] = "k_out", 0
                dve.wait_ge(*t.next("dma_in1", 11))
                if t.latest:
                    dve.wait_ge(*t.own())
                dve.tensor_tensor_scan(Z1[:, :], SCAN[:, :], LW[:, :], 0.0, ALU.mult, ALU.add).then_inc(*t.made("k_scan"))
                tt(LW[:, :], Z1[:, :], LW[:, :], ALU.subtract, "k_excl")
                dve.wait_ge(*t.at("k_sums", 4))
                dve.wait_ge(*t.next("k_sq"))
                ts(row4(X2[:, :]), sum4(), 1e-24, None, ALU.max, ALU.bypass, "k_max")
                dve.wait_ge(*t.next("k_rn"))
                tt(X1[:, :], X1[:, :], X2[:, :], ALU.mult, "k_elem")
                tt(X2[:, :], X1[:, :], AA[:, :], ALU.mult, "k_elem")
                ts(AA[:, :], AA[:, :], -1.0, PP[:, 1:2], ALU.add, ALU.mult, "k_elem")
                stt(KK[:, :], AA[:, :], 1.0, KK[:, :], ALU.add, ALU.mult, "k_elem")
                stt(AA[:, :], RR[:, :], PP[:, 2:3], KK[:, :], ALU.mult, ALU.mult, "k_prep")
                dve.wait_ge(*t.next("k_exp", 3))
                for h in range(HEADS):
                    stt(AR[HALF[h], :, 0, h, :], chunks(X1[HALF[h], :]), -1.0, chunks(LW[HALF[h], :]), ALU.mult, ALU.mult, "k_elem")
                    tt(AR[HALF[h], :, 1, h, :], chunks(RR[HALF[h], :]), Z2[HALF[h], :, :], ALU.mult, "k_elem")
                tt(BK[:, :, 0, :], chunks(X2[:, :]), chunks(Z1[:, :]), ALU.mult, "k_elem")
                tt(BK[:, :, 1, :], chunks(KK[:, :]), chunks(Z1[:, :]), ALU.mult, "k_bk")
                dve.wait_ge(*t.at("k_sums", 8))
                tt(row4(BON[:, :]), sum4(), row4(VV[:, CHUNK:]), ALU.mult, "k_bonus")
                for i, (a, b) in enumerate(NTR):
                    dve.wait_ge(*t.at("k_tr", 2 * i + 2))
                    copy(UV[HALF[1], a:b, :, :].rearrange("p n h c -> p (n h c)"), PS[HALF[1], 1, 0:(b - a) * P], "k_vt")
                batch = lambda i, a, b: PS[:, 4 + i, 0:(b - a) * CHUNK].rearrange("p (n c) -> p n c", c=CHUNK)
                for i, (a, b) in enumerate(NG):
                    dve.wait_ge(*t.next("k_g"))
                    n = (b - a) * HEADS
                    raw = PS[:, i % 2, 0:n * P].rearrange("p (n c) -> p n c", c=P)
                    for h in range(HEADS):
                        tt(LT[HALF[h], a:b, h, :], raw[HALF[0], h:n:HEADS, 0:CHUNK],
                           ML[HALF[0]].unsqueeze(1).to_broadcast([CHUNK, b - a, CHUNK]), ALU.mult, "k_lt")
                    tt(G[:, a:b, :, :].rearrange("p n h c -> p (n h) c"), raw,
                       MG.unsqueeze(1).to_broadcast([P, n, P]), ALU.mult, "k_gm")
                for level in range(LEVELS):
                    for i, (a, b) in enumerate(BATCHES):
                        dve.wait_ge(*t.next("k_a"))
                        tt(AS[:, a:b, :], batch(i, a, b), LV[:, level, :].unsqueeze(1).to_broadcast([P, b - a, CHUNK]),
                           ALU.mult, "k_am")
                        if level == 0:
                            tt(MS[:, a:b, :], AS[:, a:b, :], IST[:, :].unsqueeze(1).to_broadcast([P, b - a, CHUNK]),
                               ALU.add, "k_ms")
                    for i, (a, b) in enumerate(BATCHES if level else []):
                        dve.wait_ge(*t.next("k_mm"))
                        tt(MS[:, a:b, :], batch(i, a, b), MS[:, a:b, :], ALU.add, "k_ms")
                for c in range(NCH):
                    pc = Z2[:, c, CHUNK - 1:CHUNK]
                    if c == NCH - 1:
                        dve.wait_ge(*t.next("dma_in2", 2))
                    if c:
                        S = SIN if c == NCH - 1 else SS[(c - 1) % 2]
                        ts(SPC[:, :], S[:, :], pc, None, ALU.mult, ALU.bypass, "k_scale")
                    dve.wait_ge(*t.next("k_sa"))
                    copy(UV[HALF[0], c, 0, :], PS[HALF[0], 3, 0:CHUNK], "k_sa0")
                    dve.wait_ge(*t.next("k_sp"))
                    out, new = SS[c % 2][:, :], PS[:, 4, 0:CHUNK]
                    if c == 0:
                        dve.wait_ge(*t.at("dma_state", 0))
                        ts(out, new, pc, None, ALU.mult, ALU.bypass, "k_s")
                    else:
                        stt(out, new, pc, SPC[:, :], ALU.mult, ALU.add, "k_s")
                dve.wait_ge(*t.at("k_sums", 12))
                stt(row4(X1[:, :]), sum4(), -1.0 / CHUNK, row4(flat(Y[:, :, :])), ALU.mult, ALU.add, "k_cent")
                dve.wait_ge(*t.next("k_grs"))
                tt(X1[:, :], X1[:, :], X2[:, :], ALU.mult, "k_norm")
                ts(X1[:, :], X1[:, :], PQ[:, 0:1], PQ[:, 1:2], ALU.mult, ALU.add, "k_norm")
                tt(X1[:, :], X1[:, :], BON[:, :], ALU.add, "k_norm")
                dve.wait_ge(*t.next("dma_gg", 2))
                tt(GG[:, :], X1[:, :], GG[:, :], ALU.mult, "k_out")
                t.leave(KT)
            dve.wait_ge(*t.at("dma_m", KT))
            fill(T[:, 4:6, SEQ:SAMPLE], 0.0, "m_clear")
            fill(T[:, 0:2, 0:PAD], 0.0, "pads")
            m = M_OUT
            take_all(m, True)
            m += KT
            h_rows("ffn1", 9 * KT)
            m += 1
            m = ffn(m, FFN_TURNS + 1)
            h_rows("final", 0)


HEAD = dict(dma_in1=11, dma_in2=2, dma_gg=2, dma_state=2, k_kk=1, k_sq=1, k_sums=16, k_max=1, k_ln=1, k_rn=1, k_elem=9,
            k_scan=1, k_excl=1, k_exp=3, k_prep=1, k_bonus=1, k_bk=1, k_tr=2 * len(NTR), k_bkt=len(NTR), k_vt=len(NTR),
            k_g=len(NG), k_gm=len(NG), k_lt=2 * len(NG), k_a=3 * LEVELS, k_am=3 * LEVELS, k_mm=3 * (LEVELS - 1),
            k_ms=3 * LEVELS, k_mt=3 * LEVELS, k_nd=6 * LEVELS, k_rhs=NCH, k_rhss=NCH, k_sa=NCH, k_sa0=NCH, k_sa1=NCH,
            k_sp=NCH, k_scale=NCH - 1, k_s=NCH, k_y=NCH, k_ys=NCH, k_cent=1, k_csq=1, k_gln=1, k_grs=1, k_norm=3, k_out=1)

INPUTS = dict(weights=(N_TILES, P, D), vectors=(P, NV), consts=(P, C_END), xT=(KT, P, COLS), gates=(KT, P, 2, P),
              ffn_vec=(2, STEPS, P, 4, 6), pair_vec=(2, KT, P, 4), wkv=(KT, P, CHUNK))
OUTPUTS = dict(yT=(KT, P, COLS), small=(P, KT, 10), ffn_state=(2, STEPS, P, 4, 2, 2), wkv_out=(2, KT, P, CHUNK))


def blocks(w, rows, cols):
    return np.stack([w[r * P:(r + 1) * P, c * P:(c + 1) * P] for r, c in zip(rows, cols)], 1)


def up_tile(w, f):
    return blocks(w, range(KT), [f] * KT)


def down_tiles(w, g):
    return [blocks(w, [2 * g + k for _ in range(4) for k in range(2)], [4 * t + d for d in range(4) for _ in range(2)])
            for t in range(2)]


def constants():
    r = np.arange(P)
    s, half = r % CHUNK, r // CHUNK
    c = np.zeros((P, C_END), np.float32)
    c[:, C_ONES:C_ONES + P] = 1
    c[:, C_BD:C_BD + P] = half[:, None] == half[None, :]
    c[:, C_ID:C_ID + P] = np.eye(P)
    upto, before = s[:, None] <= s[None, :], s[:, None] < s[None, :]
    is_a, is_k = half[None, :] == 0, half[:, None] == 1
    c[:, C_MG:C_MG + P] = np.where(is_a, before & is_k, upto)
    q = np.arange(CHUNK)
    c[:, C_ML:C_ML + CHUNK] = s[:, None] < q[None, :]
    for level in range(LEVELS):
        n = 1 << level
        same = s[:, None] // (2 * n) == q[None, :] // (2 * n)
        c[:, C_LV + level * CHUNK:C_LV + (level + 1) * CHUNK] = same & (s[:, None] & n != 0) & (q[None, :] & n == 0)
    c[:, C_IST:C_IST + CHUNK] = s[:, None] == q[None, :]
    c[:, C_SCAN:] = np.arange(PACK)[None, :] % CHUNK != 0
    return c


def layout(a):
    f = lambda name: np.asarray(a[name])
    up, dn = f("ffn_w_up"), f("ffn_w_down")
    tiles = []
    wy, wx, wo = f("lru_w_y")[0], f("lru_w_x")[0], f("lru_w_out")[0]
    for g in range(LRU_GROUPS + 1):
        if g < LRU_GROUPS:
            tiles += [up_tile(wy, 2 * g), up_tile(wx, 2 * g), up_tile(wy, 2 * g + 1), up_tile(wx, 2 * g + 1)]
        if g:
            tiles += down_tiles(wo, g - 1)

    def ffn(layer):
        out = []
        for s in range(STEPS + 1):
            if s < STEPS:
                for q in (2 * s, FT + 2 * s, 2 * s + 1, FT + 2 * s + 1):
                    out.append(up_tile(up[layer], q))
            if s:
                out += down_tiles(dn[layer], s - 1)
        return out

    tiles += ffn(0)
    lora = np.concatenate([f("rw_w1")[0], f("rw_a1")[0]], 1)
    z = np.zeros((CHUNK, D), lora.dtype)
    tiles += [up_tile(lora, 0), up_tile(lora, 0), up_tile(f("rw_g1")[0], 0)]
    for w in (np.concatenate([f("rw_w2")[0], z]), np.concatenate([z, f("rw_a2")[0]]), f("rw_g2")[0]):
        tiles.append(blocks(w, [0] * KT, range(KT)))
    for name in ("rw_w_r", "rw_w_k", "rw_w_v", "rw_w_o"):
        tiles += [up_tile(f(name)[0], q) for q in range(KT)]
    tiles += ffn(1)
    weights = np.stack(tiles).reshape(N_TILES, P, D)

    col = lambda v: np.asarray(v).reshape(KT, P).T
    conv, mu = f("lru_conv_w")[0], f("rw_mu")[0]
    vecs = dict(mix0=f("norm_mix")[0], mix1=f("norm_mix")[1], ffn0=f("norm_ffn")[0], ffn1=f("norm_ffn")[1],
                final=f("norm_final"), b_x=f("lru_b_x")[0], b_y=f("lru_b_y")[0], cb=f("lru_conv_b")[0],
                ga_b=f("lru_ga_b")[0], gx_b=f("lru_gx_b")[0], lam=f("lru_lambda")[0], b_out=f("lru_b_out")[0],
                h0=f("state_lru_h")[0, 0], shift=f("state_rwkv_shift")[0, 0], w0=f("rw_w0")[0], a0=f("rw_a0")[0])
    vecs |= {f"cw{j}": conv[j] for j in range(4)} | {f"lc{j}": f("state_lru_conv")[0, 0, j] for j in range(3)}
    vecs |= {f"mu{j}": mu[j] for j in range(6)}
    vectors = np.concatenate([col(vecs[name]) for name in VEC], 1)

    xT = np.zeros((D, COLS), np.float32)
    xT[:, :SEQ] = f("x_prompt")[0].T
    xT[:, SAMPLE:] = f("x_sample")[0].T
    gates = np.stack([f("lru_ga_w")[0], f("lru_gx_w")[0]], 2)
    v = np.concatenate([f("ffn_conv_w"), f("ffn_conv_b")[:, None], f("state_ffn_conv")[:, 0]], 1)
    v = v.reshape(2, 6, 2, STEPS, 2, P).transpose(0, 3, 5, 4, 2, 1).reshape(2, STEPS, P, 4, 6)
    zero = np.zeros(D, np.float32)
    pair = np.stack([np.stack([w.reshape(KT, P) for w in ws], -1) for ws in (
        (f("rw_k_k")[0], f("rw_k_a")[0], f("rw_r_k")[0].reshape(-1), zero), (f("rw_ln_w")[0], f("rw_ln_b")[0], zero, zero))])
    wkv = f("state_rwkv_wkv")[0, 0].transpose(0, 2, 1).reshape(KT, P, CHUNK)
    return dict(weights=weights, vectors=vectors, consts=constants(), xT=xT.reshape(KT, P, COLS), gates=gates,
                ffn_vec=v, pair_vec=pair, wkv=wkv)


def outputs(r):
    y = r["yT"].reshape(D, COLS).T
    small = r["small"].transpose(2, 1, 0).reshape(10, D)
    fs = r["ffn_state"].reshape(2, STEPS, P, 2, 2, 2, 2).transpose(5, 0, 6, 4, 1, 3, 2).reshape(2, 2, 1, 2, 2 * FF)
    wkv = r["wkv_out"].reshape(2, 1, 1, KT * HEADS, CHUNK, CHUNK).transpose(0, 1, 2, 3, 5, 4)
    streams = [(small[None, None, 3 * s:3 * s + 3], small[None, 6 + s:7 + s], small[None, 8 + s:9 + s], wkv[s], fs[s])
               for s in range(2)]
    out = (y[None, :SEQ], y[None, SAMPLE:]) + streams[0] + streams[1]
    return tuple(np.ascontiguousarray(x) for x in out)


def kernel(**inputs):
    import concourse.bacc as bacc
    from concourse.bass_utils import run_bass_kernel_spmd

    arrays = {k: np.ascontiguousarray(v) for k, v in layout(inputs).items()}
    nc = bacc.Bacc("TRN2", target_bir_lowering=False, num_devices=1)
    io = {k: nc.dram_tensor(k, list(s), F32, kind="ExternalInput").ap() for k, s in INPUTS.items()}
    io |= {k: nc.dram_tensor(k, list(s), F32, kind="ExternalOutput").ap() for k, s in OUTPUTS.items()}
    io["scratch"] = nc.dram_tensor("scratch", [6, KT, P, COLS], F32, kind="Internal").ap()
    io["scratch_m"] = nc.dram_tensor("scratch_m", [KT, P, PACK], F32, kind="Internal").ap()
    build(nc, io)
    return outputs(run_bass_kernel_spmd(nc, [arrays], core_ids=[0]).results[0])
```

```python
from contextlib import ExitStack

import numpy as np

import concourse.bass as bass
from concourse import mybir

ALU = mybir.AluOpType
ACT = mybir.ActivationFunctionType
F32 = mybir.dt.float32
F32R = mybir.dt.float32r

P = 128
D = 1024
KT = D // P
SEQ, DEC = 1024, 64
GAP = 4
SAMPLE = SEQ + GAP
COLS = SAMPLE + DEC
HIST = SAMPLE - 1
CH = 3
CW = COLS // CH
PAD = 4
ROW = PAD + COLS
CHUNK = 64
NCH = (SEQ + DEC) // CHUNK
PACK = NCH * CHUNK
SUMW = PACK // 4
HEADS = 2
FF = 3 * D
FT = FF // P
STEPS = FT // 2
BATCHES = [(0, 6), (6, 12), (12, 17)]
NB = len(BATCHES)
JOBS = KT * NB
BW = 6 * CHUNK
LEVELS = 6
RMS_EPS, GN_EPS = 1e-6, 64e-5
DECAY = float(np.exp(-0.5))
LNS = 20

LRU_GROUPS = KT // 2
N_LRU = 3 * KT
N_FFN = 2 * FT + FT
N_PROJ = 6 + 3 * KT
N_OUT = KT
N_TILES = N_LRU + 2 * N_FFN + N_PROJ + N_OUT

VEC = ["mix0", "mix1", "ffn0", "ffn1", "final", "b_x", "b_y", "cw0", "cw1", "cw2", "cw3", "cb",
       "ga_b", "gx_b", "lam", "b_out", "h0", "lc0", "lc1", "lc2", "shift",
       "mu0", "mu1", "mu2", "mu3", "mu4", "mu5", "w0", "a0"]
VAT = {name: n * KT for n, name in enumerate(VEC)}
NV = len(VEC) * KT
C_ONES, C_BD, C_ID, C_MG, C_ML, C_LV, C_IST, C_SCAN = 0, 128, 256, 384, 512, 576, 960, 1024
C_END = C_SCAN + BW


PRIMED = ("dma_fs1", "dma_m1", "dma_m2", "dma_state")


class Tally:

    def __init__(self, eng, sems):
        self.eng, self.sems = eng, sems
        self.n, self.latest, self.turn, self.per = {}, None, None, {}

    def at(self, name, n):
        unit = 16 if name.startswith("dma_") else 1
        n += name in PRIMED
        assert n > 0, name
        per = self.per.get(name, 0) if self.turn is not None else 0
        return self.sems[name], self.turn * (unit * per) + unit * n if per else unit * n

    def next(self, name, k=1):
        self.n[name] = self.n.get(name, 0) + k
        return self.at(name, self.n[name])

    def own(self):
        return self.at(self.latest, self.n[self.latest])

    def made(self, name, n=None):
        self.n[name] = self.n.get(name, 0) + 1 if n is None else n
        self.latest = name
        return self.sems[name], 16 if name.startswith("dma_") else 1

    def enter(self, turn, per):
        self.turn, self.per, self.start = turn, per, dict(self.n)

    def leave(self, turns):
        for k, v in self.n.items():
            got = v - self.start.get(k, 0)
            if k in ("taken0", "taken1"):
                self.n[k] += self.per.get(k, 0) * (turns - 1)
                continue
            assert got in (0, self.per.get(k, 0)), (self.eng, k, got)
            if got:
                self.n[k] = self.start.get(k, 0) + got * turns
        self.turn, self.per = None, {}


FFN_TURN = dict(w_lo=12, w_hi=12, dma_w0=6, dma_w1=6, conv=8, hist=8, kept=8, tap=16, gelu=4, p_full=4, p_hi=4,
                p_lo=4, dma_fp0=1, dma_fp1=1, dma_fs0=1, dma_fs1=1, acc_ready=24, taken0=12, taken1=12)
FFN_TURNS = (STEPS - 2) // 2
MIXES = [1, 4, 5, 0, 2, 3]
M_LRU = 1
M_N1 = M_LRU + 4 * KT + LRU_GROUPS * KT
M_FFN1 = M_N1 + 1
M_N2 = M_FFN1 + 2 * FT + STEPS * KT
M_PROJ = M_N2 + 1
M_OUT = M_PROJ + 3 + 6 * KT
M_N3 = M_OUT + KT
M_FFN2 = M_N3 + 1
M_N4 = M_FFN2 + 2 * FT + STEPS * KT
H_FINAL = 9 * KT
W_FFN1 = N_LRU
W_PROJ = W_FFN1 + N_FFN
W_OUT = W_PROJ + N_PROJ
W_FFN2 = W_OUT + N_OUT


def groups(b, size):
    a, z = BATCHES[b]
    return [(c, min(c + size, z)) for c in range(a, z, size)]


def build(nc, io):
    ctx = ExitStack()
    with ctx:
        base = -(-nc.sbuf_base // 64) * 64

        def at(name, shape, offset, dt=F32):
            return nc.alloc_sbuf_tensor_at(name, [P] + shape, dt, offset=base + offset)

        x_at = 0
        h_at = x_at + KT * COLS * 4
        p_at = h_at + 2 * KT * COLS * 4
        t_at = p_at + KT * ROW * 4
        w_at = t_at + 8 * ROW * 4
        c_at = w_at + 24576
        X = at("X", [KT, COLS], x_at)
        HH = at("HH", [KT, COLS], h_at, F32R)
        HL = at("HL", [KT, COLS], h_at + KT * COLS * 4, F32R)
        PH = at("PH", [4, COLS], p_at, F32R)
        PL = at("PL", [4, COLS], p_at + 4 * COLS * 4, F32R)
        HF = at("HF", [KT, ROW], p_at)
        T = at("T", [8, ROW], t_at)
        TR = at("TR", [4, ROW], t_at, F32R)
        RAW = [at(f"RAW{s}", [KT, P], w_at + 4096 * s) for s in range(2)]
        WH = [at(f"WH{s}", [KT, P], w_at + 8192 + 8192 * s, F32R) for s in range(2)]
        WL = [at(f"WL{s}", [KT, P], w_at + 12288 + 8192 * s, F32R) for s in range(2)]
        o = c_at
        CO = at("CO", [C_LV], o); o += C_LV * 4
        V = at("V", [NV], o); o += NV * 4
        DV = at("DV", [14, KT], o); o += 14 * KT * 4
        GW = [at(f"GW{s}", [2, P], o + 1024 * s) for s in range(2)]; o += 2048
        FP = [at(f"FP{s}", [4, 6], o + 96 * s) for s in range(2)]; o += 192
        FS = [at(f"FS{s}", [4, 2, 2], o + 64 * s) for s in range(2)]; o += 128
        ST = at("ST", [KT, 10], o); o += KT * 10 * 4
        PP = [at(f"PP{b}", [4], o + 32 * b) for b in range(NB)]; o += 96
        PQ = [at(f"PQ{b}", [4], o + 32 * b) for b in range(NB)]; o += 96
        SR = at("SR", [ROW], o); o += ROW * 4
        PRIME = at("PRIME", [len(PRIMED), 2], o); o += 64
        assert o + base <= nc.sbuf_usable_end, (o + base, nc.sbuf_usable_end)
        o = h_at
        AR = at("AR", [NCH, 2, HEADS, CHUNK], o); o += NCH * 1024
        G = at("G", [NCH, HEADS, 2 * CHUNK], o); o += NCH * 1024
        ND = at("ND", [NCH, HEADS, CHUNK], o); o += NCH * 512
        LT = at("LT", [NCH, HEADS, CHUNK], o); o += NCH * 512
        UV = at("UV", [NCH, HEADS, CHUNK], o); o += NCH * 512
        BKT = at("BKT", [NCH, P], o); o += NCH * 512
        assert o <= p_at
        o = p_at
        BK = at("BK", [NCH, 2, CHUNK], o); o += NCH * 512
        AS = at("AS", [NCH, CHUNK], o); o += PACK * 4
        MS = at("MS", [NCH + 1, CHUNK], o); o += (PACK + CHUNK) * 4
        Y = at("Y", [NCH, CHUNK], o); o += PACK * 4
        BON = at("BON", [PACK], o); o += PACK * 4
        Z1 = at("Z1", [PACK], o); o += PACK * 4
        Z2 = at("Z2", [NCH, CHUNK], o); o += PACK * 4
        assert o <= t_at
        o = t_at
        LW = at("LW", [PACK], o); o += PACK * 4
        AA = at("AA", [PACK], o); o += PACK * 4
        GG = at("GG", [PACK], o); o += PACK * 4
        RR = at("RR", [PACK], o); o += PACK * 4
        KK = at("KK", [PACK], o); o += PACK * 4
        X1 = at("X1", [PACK], o); o += PACK * 4
        X2 = at("X2", [PACK], o); o += PACK * 4
        X3 = at("X3", [PACK], o); o += PACK * 4
        assert o <= w_at
        o = w_at + 8192
        VV = at("VV", [PACK + CHUNK], o); o += (PACK + CHUNK) * 4
        LV = at("LV", [LEVELS, CHUNK], o); o += LEVELS * CHUNK * 4
        IST = at("IST", [CHUNK], o); o += CHUNK * 4
        SCAN = at("SCAN", [BW], o); o += BW * 4
        Q1 = at("Q1", [PACK], o); o += PACK * 4
        SE = [at(f"SE{s}", [CHUNK], o + 256 * s) for s in range(2)]; o += 512
        SS = [at(f"SS{s}", [CHUNK], o + 256 * s) for s in range(2)]; o += 512
        SPC = at("SPC", [CHUNK], o); o += 256
        RHS = at("RHS", [CHUNK], o); o += 256
        SIN = at("SIN", [CHUNK], o); o += 256
        assert o <= c_at, (o, c_at)

        PS = ctx.enter_context(nc.psum_tensor("PS", [P, 8, 512], F32))
        ACC = [PS[:, 0:3, 0:CW], PS[:, 3:6, 0:CW]]

        names = """dma_w0 dma_w1 dma_const dma_x0 dma_x1 dma_x2 dma_x3 dma_x4 dma_x5 dma_x6 dma_x7 dma_gw0 dma_gw1 dma_fp0 dma_fp1 dma_fs0 dma_fs1
            dma_spill0 dma_spill1 dma_spill2 dma_in0 dma_in1 dma_in2 dma_pq0 dma_pq1 dma_pq2 dma_sin dma_const2 dma_state
            dma_m0 dma_m1 dma_m2 dma_load0 dma_load1 dma_load2 dma_load3
            dma_y0 dma_y1 dma_st
            w_hi w_lo acc_ready taken0 taken1 pads vprep absv hist kept tap conv gelu squared summed rstd
            h_full h_hi h_lo h_lo1 h_used mixhalf hf p_full p_hi p_lo tan root post
            lora lora_hi lora_lo zeroed m_clear
k_kk k_sq s_kk k_max k_ln k_rn k_scan k_excl k_ez2 k_elw k_ez1 k_arr k_ar k_ka k_k2 k_prep k_kn k_b k_bk1
            k_bk s_bon k_bonus k_tb k_tv k_bkt k_vt k_g k_gm k_lt k_a k_am k_mm k_ms k_mt k_nd k_rhs k_rhss k_sa k_uv
            k_sp k_scale k_s k_y k_ys s_mean k_cent k_csq s_var k_gln k_grs k_pn k_pt k_padd k_out""".split()
        sems = {n: ctx.enter_context(nc.semaphore(n)) for n in names}

        def vec(name, k):
            c = VAT[name] + k
            return V[:, c:c + 1]

        ONES, BD, ID = CO[:, 0:P], CO[:, C_BD:C_BD + P], CO[:, C_ID:C_ID + P]
        MG, ML = CO[:, C_MG:C_MG + P], CO[:, C_ML:C_ML + CHUNK]
        HALF = [slice(0, CHUNK), slice(CHUNK, P)]
        scr, scrm = io["scratch"], io["scratch_m"]

        def flat(t):
            return t[:, :, :].rearrange("p n c -> p (n c)")

        def mix_row(i):
            return i % 4 if i < 3 * KT else 4 + i % 2 if i < 4 * KT else i % KT % 6

        def row3(t):
            return t.rearrange("p (j c) -> p j c", j=CH)

        def tails(t, keep):
            w = COLS - SEQ
            return t[:, SEQ - w:COLS].rearrange("p (s c) -> p s c", s=2)[:, :, w - keep:w]

        def chunks(t):
            return t.rearrange("p (n c) -> p n c", c=CHUNK)

        def pick(t, turn, plus=0):
            if turn is None:
                return t[plus]
            names = " ".join("abcde"[:len(t.shape) - 2])
            return t[bass.ds(turn + plus, 1)].rearrange(f"o p {names} -> (o p) {names}")

        block = ctx.enter_context(nc.Block())

        @block.sync
        def _(sp):
            t = Tally(sp, sems)

            def weight(n, turn=None):
                s = n % 2
                if n >= 2:
                    sp.wait_ge(*t.at("w_lo", n - 1))
                src = io["weights"][n] if turn is None else pick(io["weights"], turn * 12, n)
                sp.dma_start(RAW[s][:, :, :].rearrange("p k c -> p (k c)"), src).then_inc(*t.made(f"dma_w{s}"))

            for j, name in enumerate(PRIMED):
                sp.dma_start(PRIME[:, j, :], io["consts"][:, 0:2]).then_inc(sems[name], 16)
            sp.dma_start(V[:, :], io["vectors"]).then_inc(*t.made("dma_const"))
            sp.dma_start(CO[:, :], io["consts"][:, 0:C_LV]).then_inc(*t.made("dma_const"))
            for k in range(KT):
                sp.dma_start(X[:, k, :], io["xT"][k]).then_inc(*t.made(f"dma_x{k}"))
            weight(0)
            weight(1)
            n = 2
            for g in range(LRU_GROUPS + 1):
                if g < LRU_GROUPS:
                    for f in (2 * g, 2 * g + 1):
                        if f >= 2:
                            sp.wait_ge(*t.at("root", f - 1))
                        sp.dma_start(GW[f % 2][:, :, :], io["gates"][f]).then_inc(*t.made(f"dma_gw{f % 2}"))
                while n < min(N_LRU, 4 + 6 * g) + 2:
                    weight(n)
                    n += 1

            def ffn(layer, first, convs):
                def step(s, tiles, turn=None):
                    b = s % 2
                    if s:
                        sp.wait_ge(*t.at("conv", convs + 4 * (s - 1)))
                    src = io["ffn_vec"][layer, s] if turn is None else pick(io["ffn_vec"][layer], turn * 2, s)
                    sp.dma_start(FP[b][:, :, :], src).then_inc(*t.made(f"dma_fp{b}"))
                    if s >= 1:
                        keep(s - 1, turn)
                    for q in tiles:
                        weight(q, turn)

                def keep(s, turn=None):
                    sp.wait_ge(*t.next("kept", 4))
                    dst = io["ffn_state"][layer, s] if turn is None else pick(io["ffn_state"][layer], turn * 2, s)
                    sp.dma_start(dst, FS[s % 2][:, :, :, :]).then_inc(*t.made(f"dma_fs{s % 2}"))

                t.n["kept"] = convs_kept[layer]
                w = first + 2
                step(0, range(w, w + 4))
                w += 4
                with sp.Fori(0, FFN_TURNS) as turn:
                    t.enter(turn, FFN_TURN)
                    step(1, range(w, w + 6), turn)
                    step(2, range(w + 6, w + 12), turn)
                    t.leave(FFN_TURNS)
                w += 12 * FFN_TURNS
                step(STEPS - 1, range(w, w + 6))
                keep(STEPS - 1)
                for q in range(w + 6, w + 8):
                    if q < N_TILES:
                        weight(q)

            convs_kept = [2 * KT, 2 * KT + 2 * FT]
            ffn(0, W_FFN1, KT)
            for q in range(W_PROJ + 2, W_OUT):
                weight(q)
            sp.wait_ge(*t.at("acc_ready", M_OUT))
            sp.wait_ge(*t.at("h_lo", 8 * KT // 2))
            sp.wait_ge(*t.at("h_lo1", 8 * KT // 2))
            weight(W_OUT)
            weight(W_OUT + 1)
            for name in ("dma_spill0", "dma_spill1", "dma_spill2"):
                sp.wait_ge(*t.at(name, 2 * KT))
            for tile, a, b in ((LV[:, :, :].rearrange("p l c -> p (l c)"), C_LV, C_IST),
                               (IST[:, :], C_IST, C_SCAN), (SCAN[:, :], C_SCAN, C_END)):
                sp.dma_start(tile, io["consts"][:, a:b]).then_inc(*t.made("dma_const2"))

            def load(b, turn, f, tile, j, event):
                a, z = BATCHES[b][0] * CHUNK, BATCHES[b][1] * CHUNK
                src = pick(scr[j], turn, f)
                sp.dma_start(tile[:, a:min(z, SEQ)], src[:, a:min(z, SEQ)]).then_inc(*t.made(event))
                if z > SEQ:
                    sp.dma_start(tile[:, SEQ:z], src[:, SAMPLE:COLS]).then_inc(*t.made(event))

            def interval(job, turn=None):
                if job + 2 < JOBS:
                    f, b = divmod(job + 2, NB)
                    sp.dma_start(PP[b][:, :], pick(io["pair_vec"][0], turn, f)).then_inc(*t.made(f"dma_in{b}"))
                    for tile, j in ((KK, 4), (LW, 0), (AA, 1), (RR, 3), (VV, 5)):
                        load(b, turn, f, tile, j, f"dma_in{b}")
                if 0 <= job < JOBS:
                    f, b = divmod(job, NB)
                    if job:
                        sp.wait_ge(*t.at(f"dma_m{b}", f))
                    sp.dma_start(PQ[b][:, :], pick(io["pair_vec"][1], turn, f)).then_inc(*t.made(f"dma_pq{b}"))
                    load(b, turn, f, GG, 2, f"dma_pq{b}")
                    if b == NB - 1:
                        sp.dma_start(SIN[:, :], pick(io["wkv"], turn, f)).then_inc(*t.made("dma_sin"))
                if job >= 1:
                    f, b = divmod(job - 1, NB)
                    a, z = BATCHES[b][0] * CHUNK, BATCHES[b][1] * CHUNK
                    sp.wait_ge(*t.next("k_out"))
                    sp.dma_start(pick(scrm, turn, f)[:, a:z], GG[:, a:z]).then_inc(*t.made(f"dma_m{b}"))
                    if b == NB - 1:
                        sp.wait_ge(*t.next("k_s", NCH))
                        for q in range(2):
                            dst = pick(io["wkv_out"][q], turn, f)
                            sp.dma_start(dst, SE[q][:, :]).then_inc(*t.made("dma_state"))

            for job in (-2, -1, 0):
                interval(job)
            sp.wait_ge(*t.at("k_g", 3))
            sp.wait_ge(*t.at("k_bonus", 1))
            with sp.Fori(0, KT - 1) as turn:
                t.enter(turn, HEAD_TURN)
                for job in (1, 2, 3):
                    interval(job, turn)
                t.leave(KT - 1)
            def result(k):
                b = k % 4
                sp.dma_start(T[:, 4 + b, 0:SEQ], scrm[k][:, 0:SEQ]).then_inc(*t.made(f"dma_load{b}"))
                sp.dma_start(T[:, 4 + b, SAMPLE:COLS], scrm[k][:, SEQ:PACK]).then_inc(*t.made(f"dma_load{b}"))

            interval(JOBS - 2)
            interval(JOBS - 1)
            sp.wait_ge(*t.at("m_clear", 1))
            for b in range(NB):
                sp.wait_ge(*t.at(f"dma_m{b}", KT - 1))
            for k in range(4):
                result(k)
            interval(JOBS)
            for k in range(4, KT):
                sp.wait_ge(*t.at("h_lo1" if k % 2 else "h_lo", 8 * KT // 2 + k // 2 - 1))
                if k == KT - 1:
                    for b in range(NB):
                        sp.wait_ge(*t.at(f"dma_m{b}", KT))
                result(k)
            for q in range(W_OUT + 2, W_FFN2 + 2):
                weight(q)
            sp.dma_start(io["small"], ST[:, :, :]).then_inc(*t.made("dma_st"))
            ffn(1, W_FFN2, KT + 2 * FT)
            for k in range(KT):
                sp.wait_ge(*t.at("h_full", H_FINAL + k + 1))
                sp.dma_start(io["yT"][k], T[:, 4 + k % 2, 0:COLS]).then_inc(*t.made(f"dma_y{k % 2}"))
            for name in ("dma_y0", "dma_y1", "dma_st", "dma_fs0", "dma_fs1"):
                sp.wait_ge(*t.at(name, t.n[name]))
            sp.wait_ge(*t.at("dma_state", 2 * KT))

        @block.scalar
        def _(act):
            t = Tally(act, sems)

            def run(out, in_, func, event, bias=0.0, scale=1.0, n=None):
                if t.latest:
                    act.wait_ge(*t.own())
                act.activation(out, in_, func, bias=bias, scale=scale).then_inc(*t.made(event, n))

            def w_hi(n, ready):
                if n >= N_TILES:
                    return
                act.wait_ge(*t.next(f"dma_w{n % 2}"))
                if ready:
                    act.wait_ge(*t.at("acc_ready", ready))
                run(WH[n % 2][:, :, :], RAW[n % 2][:, :, :], ACT.Copy, "w_hi")

            def evacuate(m, out, func, bias=0.0, scale=1.0):
                act.wait_ge(*t.at("acc_ready", m + 1))
                run(out, ACC[m % 2], func, f"taken{m % 2}", bias, scale, m // 2 + 1)

            def norm(m, source, n=None, weights=None):
                for k in range(KT):
                    if weights == "two" and k == KT // 2:
                        w_hi(n, m - KT // 2)
                    if weights == "each":
                        w_hi(n + k, m - KT + k + 1)
                    source(k)
                    if k >= 3:
                        act.wait_ge(*t.at("summed", t.n.get("squared", 0) // KT * (KT - 1) + k - 2))
                    run(T[:, 3 if k == 0 else 4 + k % 2, 0:COLS], X[:, k, :], ACT.Square, "squared")
                if weights == "both":
                    w_hi(n, 0)
                if weights in ("both", "two"):
                    w_hi(n + 1, m)
                evacuate(m, row3(T[:, 2, 0:COLS]), ACT.Ln, bias=RMS_EPS, scale=1.0 / D)
                run(T[:, 2, 0:COLS], T[:, 2, 0:COLS], ACT.Exp, "rstd", scale=-0.5)

            def h_hi(k, source="h_full", row=None):
                if source:
                    act.wait_ge(*t.next(source))
                run(HH[:, k, :], T[:, 4 + k % 4 if row is None else row, 0:COLS], ACT.Copy, "h_hi")

            act.wait_ge(*t.at("dma_const", 2))
            lam = V[:, VAT["lam"]:VAT["lam"] + KT]
            run(DV[:, 6, :], lam, ACT.Abs, "absv")
            run(DV[:, 6, :], DV[:, 6, :], ACT.Exp, "absv", scale=-1.0)
            run(DV[:, 7, :], lam, ACT.Relu, "absv", scale=-1.0)
            norm(0, lambda k: act.wait_ge(*t.at(f"dma_x{k}", 1)), 0, "both")
            for k in range(KT):
                h_hi(k)

            UB, R, I, S = T[:, 0, PAD:ROW], T[:, 4, 0:COLS], T[:, 5, 0:COLS], T[:, 6, 0:COLS]
            m, n = M_LRU, 2

            def gates(m, f):
                evacuate(m, row3(R), ACT.Sigmoid, bias=vec("ga_b", f))
                evacuate(m + 1, row3(I), ACT.Sigmoid, bias=vec("gx_b", f))
                if f == 0:
                    act.wait_ge(*t.next("vprep"))
                run(R, R, ACT.Tanh, "tan", scale=DV[:, 8, f:f + 1])
                if f:
                    act.wait_ge(*t.at("p_lo", f))
                run(S, R, ACT.Sqrt, "root", scale=4.0)

            def p_hi(slot, src):
                act.wait_ge(*t.next("p_full"))
                run(PH[:, slot, :], src, ACT.Copy, "p_hi")

            for g in range(LRU_GROUPS):
                f = 2 * g
                slot = 2 * (g % 2)
                evacuate(m, row3(T[:, 2, 0:COLS]), ACT.Gelu_apprx_tanh, bias=vec("b_y", f))
                w_hi(n, m + 1)
                evacuate(m + 1, row3(UB), ACT.Identity, bias=vec("b_x", f))
                w_hi(n + 1, m + 2)
                evacuate(m + 2, row3(T[:, 3, 0:COLS]), ACT.Gelu_apprx_tanh, bias=vec("b_y", f + 1))
                w_hi(n + 2, m + 3)
                gates(m + 3, f)
                p_hi(slot, S)
                evacuate(m + 5, row3(UB), ACT.Identity, bias=vec("b_x", f + 1))
                w_hi(n + 3, m + 6)
                m, n = m + 6, n + 4
                if g:
                    w_hi(n, m + 4)
                    w_hi(n + 1, m + 8)
                    m, n = m + KT, n + 2
                gates(m, f + 1)
                p_hi(slot + 1, S)
                m += 2
            m += KT
            assert (m, n) == (M_N1, W_FFN1)

            def added(m0):
                return lambda k: act.wait_ge(*t.at(f"taken{(m0 + k) % 2}", (m0 + k) // 2 + 1))

            def ffn(m, n):
                def step(s, m, n):
                    for j in range(2):
                        gate = T[:, 2 + 2 * j, 0:COLS]
                        evacuate(m, row3(T[:, 0, PAD:ROW]), ACT.Copy)
                        w_hi(n, m + 1)
                        act.wait_ge(*t.next("conv"))
                        run(gate, gate, ACT.Gelu_apprx_tanh, "gelu")
                        evacuate(m + 1, row3(T[:, 1, PAD:ROW]), ACT.Copy)
                        w_hi(n + 1, m + 2)
                        act.wait_ge(*t.next("conv"))
                        p_hi(2 * (s % 2) + j, gate)
                        m, n = m + 2, n + 2
                    return m, n

                def down(m, n):
                    w_hi(n, m + 4)
                    w_hi(n + 1, m + 8)
                    return m + KT, n + 2

                m, n = step(0, m, n)
                with act.Fori(0, FFN_TURNS) as turn:
                    if t.latest:
                        act.wait_ge(*t.own())
                    t.enter(turn, FFN_TURN)
                    a, b = m, n
                    for s in (1, 2):
                        a, b = step(s, a, b)
                        a, b = down(a, b)
                    t.leave(FFN_TURNS)
                m, n = m + 24 * FFN_TURNS, n + 12 * FFN_TURNS
                m, n = step(STEPS - 1, m, n)
                m, n = down(m, n)
                return m + KT, n

            norm(m, added(m - KT), n, "two")
            for k in range(KT):
                h_hi(k)
            act.wait_ge(*t.next("conv", KT))
            m, n = ffn(M_FFN1, n + 2)
            assert (m, n) == (M_N2, W_PROJ)
            norm(m, added(m - KT), n, "two")
            n += 2

            m = M_PROJ

            halves, mixed = 0, 0

            def mix_half():
                nonlocal halves
                if halves < len(MIXES) * KT:
                    j, k = MIXES[halves // KT], halves % KT
                    before = KT + (halves - k) // 2
                    name = "h_lo1" if k % 2 else "h_lo"
                    if halves < 3 * KT:
                        if halves >= 4:
                            act.wait_ge(*t.at(name, KT + halves // 2 - 1))
                    elif halves < 4 * KT:
                        if halves >= 3 * KT + 2:
                            act.wait_ge(*t.at(name, KT + halves // 2))
                    elif k == 0:
                        act.wait_ge(*t.at("h_lo", before))
                        act.wait_ge(*t.at("h_lo1", before))
                    elif k >= 6:
                        act.wait_ge(*t.at(name, before + 1))
                    run(T[:, mix_row(halves), 0:COLS], HF[:, k, PAD:ROW], ACT.Copy, "mixhalf", scale=DV[:, j, k:k + 1])
                    halves += 1

            def mix_hi(m, k):
                nonlocal mixed
                if m is None:
                    pass
                elif k < KT - 1:
                    act.wait_ge(*t.next("h_used"))
                else:
                    act.wait_ge(*t.at("acc_ready", m + 1))
                h_hi(k, row=mix_row(mixed))
                mixed += 1
                if mixed <= 4 * KT - 2 or (mixed > 4 * KT and k in (2, 3)):
                    mix_half()

            act.wait_ge(*t.at("hf", KT + 2))
            mix_half()
            mix_half()
            for k in range(KT):
                mix_hi(None, k)
            for k in range(KT):
                mix_hi(m, k)
            lora, lora_g = T[:, 6, 0:COLS], T[:, 7, 0:COLS]
            half_acc = lambda m, h: ACC[m % 2][HALF[h]]
            act.wait_ge(*t.at("acc_ready", m + 1))
            run(row3(lora)[HALF[0]], half_acc(m, 0), ACT.Tanh, f"taken{m % 2}", n=m // 2 + 1)
            w_hi(n, m + 1)
            for k in range(KT):
                mix_hi(m + 1, k)
            act.wait_ge(*t.at("acc_ready", m + 2))
            run(row3(lora)[HALF[1]], half_acc(m + 1, 1), ACT.Copy, f"taken{(m + 1) % 2}", n=(m + 1) // 2 + 1)
            w_hi(n + 1, m + 2)
            act.wait_ge(*t.at("h_lo", KT + 3 * KT // 2))
            act.wait_ge(*t.at("h_lo1", KT + 3 * KT // 2))
            run(TR[:, 0, 0:COLS], lora, ACT.Copy, "lora_hi")
            evacuate(m + 2, row3(lora_g), ACT.Sigmoid)
            w_hi(n + 2, m + 3)
            run(TR[:, 2, 0:COLS], lora_g, ACT.Copy, "lora_hi")
            act.wait_ge(*t.at("lora_lo", 2))
            m0, m, n = m, m + 3, n + 3
            spills = 0

            def spill(m, j, f, func, bias=0.0):
                nonlocal spills
                b = spills % 3
                row = SR[:, 0:COLS] if b == 2 else T[:, 6 + b, 0:COLS]
                if spills >= 3:
                    act.wait_ge(*t.at(f"dma_spill{b}", spills // 3))
                evacuate(m, row3(row), func, bias=bias)
                if t.latest:
                    act.wait_ge(*t.own())
                act.dma_start(scr[j, f], row).then_inc(*t.made(f"dma_spill{b}"))
                t.latest = f"taken{m % 2}"
                spills += 1

            for j in range(3):
                for f in range(KT):
                    if j == 0:
                        spill(m, j, f, ACT.Sigmoid, vec("w0", f))
                    elif j == 1:
                        spill(m, j, f, ACT.Sigmoid, vec("a0", f))
                    else:
                        spill(m, j, f, ACT.Copy)
                    if j < 2 and f % 2:
                        mix_hi(m0 + 2, (KT * j + f) // 2)
                    m += 1
                w_hi(n, m)
                n += 1
            for j in range(3, 6):
                for f in range(KT):
                    if f == KT - 1 and j < 5:
                        for k in range(KT):
                            mix_hi(m, k)
                    spill(m, j, f, ACT.Copy)
                    if f < 6 and j < 5:
                        mix_half()
                    m += 1
                    if j < 5 or f < KT - 2:
                        w_hi(n, m)
                        n += 1
            assert m == M_OUT

            for b in range(3):
                act.wait_ge(*t.at(f"dma_spill{b}", 2 * KT))

            def interval(job, turn=None):
                has_s, has_l, has_p, has_n = 0 <= job < JOBS, 0 <= job + 1 < JOBS, job + 2 < JOBS, job >= 1
                a, z = BATCHES[job % NB]
                la, lz = BATCHES[(job + 1) % NB]
                pb = (job + 2) % NB
                lo, hi = BATCHES[pb][0] * CHUNK, BATCHES[pb][1] * CHUNK
                na, nz = BATCHES[(job - 1) % NB]
                q1 = Q1[:, na * CHUNK:nz * CHUNK]

                def turned_copies():
                    act.wait_ge(*t.next("k_mt"))
                    for q in range(2):
                        n = len(range(la + q, lz, 2))
                        src = PS[HALF[q], 7, 0:n * P].rearrange("p (n h c) -> p n h c", h=HEADS, c=CHUNK)
                        for h in range(HEADS):
                            run(ND[HALF[h], la + q:lz:2, h, :], src[:, :, h, :], ACT.Copy, "k_nd")

                if has_p:
                    act.wait_ge(*t.next(f"dma_in{pb}", 11 if pb == NB - 1 else 6))
                    run(X1[:, lo:hi], KK[:, lo:hi], ACT.Copy, "k_kk", scale=PP[pb][:, 0:1])
                    run(X2[:, lo:hi], X1[:, lo:hi], ACT.Square, "k_sq")
                for k in range(LEVELS):
                    c = a + k if has_s and a + k < z else None
                    if c is not None:
                        act.wait_ge(*t.next("k_rhs"))
                        run(RHS[:, :], PS[:, 0, 0:CHUNK], ACT.Copy, "k_rhss")
                    if has_l and k:
                        turned_copies()
                    if k == 0 and has_p:
                        act.wait_ge(*t.next("k_scan"))
                        run(flat(Z2)[:, lo:hi], Z1[:, lo:hi], ACT.Exp, "k_ez2", scale=-DECAY)
                    if k == 0 and has_n:
                        act.wait_ge(*t.next("k_cent"))
                        run(Q1[:, na * CHUNK:nz * CHUNK], Y[:, na:nz, :], ACT.Square, "k_csq")
                    if k == 1 and has_p:
                        act.wait_ge(*t.next("k_excl"))
                        run(LW[:, lo:hi], LW[:, lo:hi], ACT.Exp, "k_elw", scale=-DECAY)
                        run(Z1[:, lo:hi], Z1[:, lo:hi], ACT.Exp, "k_ez1", scale=DECAY)
                        act.wait_ge(*t.next("k_max"))
                        run(X2[:, lo:hi], X2[:, lo:hi], ACT.Ln, "k_ln", scale=float(2 ** LNS))
                    if k == 1 and has_n:
                        act.wait_ge(*t.next("s_var"))
                        run(q1, PS[:, 3, 0:(nz - na) * CHUNK], ACT.Ln, "k_gln", scale=1.0 / CHUNK, bias=GN_EPS)
                    if k == 2 and has_n:
                        run(q1, q1, ACT.Exp, "k_grs", scale=-0.5)
                    if k == 2 and has_p:
                        run(X2[:, lo:hi], X2[:, lo:hi], ACT.Exp, "k_rn", scale=-0.5, bias=0.5 * LNS * float(np.log(2.0)))
                    if c is not None:
                        act.wait_ge(*t.next("k_y"))
                        run(Y[:, c, :], PS[:, 1, 0:CHUNK], ACT.Copy, "k_ys")
                    if k == 3 and has_p:
                        for g, (ga, gz) in enumerate(groups(pb, 3)):
                            act.wait_ge(*t.next("k_tb"))
                            run(BKT[:, ga:gz, :], PS[:, 4 + g, 0:(gz - ga) * P].rearrange("p (n c) -> p n c", c=P), ACT.Copy, "k_bkt")
                if has_l:
                    turned_copies()

            for job in (-2, -1, 0):
                interval(job)
            with act.Fori(0, KT - 1) as turn:
                t.enter(turn, HEAD_TURN)
                for job in (1, 2, 3):
                    interval(job, turn)
                t.leave(KT - 1)
            for job in (JOBS - 2, JOBS - 1, JOBS):
                interval(job)
            w_hi(W_OUT, M_OUT)
            for k in range(KT):
                if k == 4:
                    act.wait_ge(*t.at("k_out", JOBS))
                    act.wait_ge(*t.at("dma_state", 2 * KT))
                    w_hi(W_OUT + 1, M_OUT)
                act.wait_ge(*t.next(f"dma_load{k % 4}", 2))
                h_hi(k, None)
            m, n = M_OUT + KT, W_OUT + 2
            norm(m, added(m - KT), n, "each")
            for k in range(KT):
                h_hi(k)
            m, n = ffn(M_FFN2, n + KT)
            assert (m, n) == (M_N4, N_TILES)
            norm(m, added(m - KT))

        @block.gpsimd
        def _(pool):
            t = Tally(pool, sems)

            def rest(out, full, hi, wait, event):
                pool.wait_ge(*t.next(wait))
                if t.latest:
                    pool.wait_ge(*t.own())
                pool.tensor_tensor(out, full, hi, ALU.subtract).then_inc(*t.made(event))

            n = 0

            def w_lo(k=1):
                nonlocal n
                for _ in range(k):
                    if n < N_TILES:
                        s = n % 2
                        rest(WL[s][:, :, :], RAW[s][:, :, :], WH[s][:, :, :], "w_hi", "w_lo")
                        n += 1

            def h_lo(k, row=None):
                if k % 2:
                    t.n["h_hi"] += 1
                else:
                    rest(HL[:, k, :], T[:, 4 + k % 4 if row is None else row, 0:COLS], HH[:, k, :], "h_hi", "h_lo")

            def p_lo(slot, full):
                rest(PL[:, slot, :], full, PH[:, slot, :], "p_hi", "p_lo")

            w_lo(2)
            for k in range(KT):
                h_lo(k)
            S = T[:, 6, 0:COLS]
            for g in range(LRU_GROUPS):
                slot = 2 * (g % 2)
                w_lo(3)
                p_lo(slot, S)
                w_lo(1)
                if g:
                    w_lo(2)
                p_lo(slot + 1, S)
            w_lo(2)

            def ffn():
                nonlocal n

                def step(s):
                    for j in range(2):
                        w_lo(2)
                        p_lo(2 * (s % 2) + j, T[:, 2 + 2 * j, 0:COLS])

                step(0)
                with pool.Fori(0, FFN_TURNS) as turn:
                    if t.latest:
                        pool.wait_ge(*t.own())
                    t.enter(turn, FFN_TURN)
                    for s in (1, 2):
                        step(s)
                        w_lo(2)
                    t.leave(FFN_TURNS)
                n += 12 * (FFN_TURNS - 1)
                step(STEPS - 1)
                w_lo(2)
                w_lo(2)

            for k in range(KT):
                h_lo(k)
            ffn()
            assert n == W_PROJ + 2
            for k in range(2 * KT):
                h_lo(k % KT, mix_row(k))
            w_lo()
            for k in range(KT):
                h_lo(k, mix_row(2 * KT + k))
            w_lo()
            rest(TR[:, 1, 0:COLS], T[:, 6, 0:COLS], TR[:, 0, 0:COLS], "lora_hi", "lora_lo")
            w_lo()
            rest(TR[:, 3, 0:COLS], T[:, 7, 0:COLS], TR[:, 2, 0:COLS], "lora_hi", "lora_lo")
            for k in range(KT):
                h_lo(k, mix_row(3 * KT + k))
                if k % 4 == 3:
                    w_lo()
            w_lo()
            for j in range(3):
                for f in range(KT):
                    if f == KT - 1 and j < 2:
                        for k in range(KT):
                            h_lo(k, mix_row((j + 4) * KT + k))
                    if j < 2 or f < KT - 2:
                        w_lo()
            assert n == W_OUT
            pool.wait_ge(*t.at("acc_ready", M_OUT))
            for z in (AR[:, :, :, :, :], ND[:, :, :, :], LT[:, :, :, :], UV[:, :, :, :], VV[:, PACK:], MS[:, NCH, :]):
                if t.latest:
                    pool.wait_ge(*t.own())
                pool.memset(z, 0.0).then_inc(*t.made("zeroed"))

            def tt(out, x, y, op, event):
                pool.wait_ge(*t.own())
                pool.tensor_tensor(out, x, y, op).then_inc(*t.made(event))

            def interval(job, turn=None):
                has_p, has_n = job + 2 < JOBS, job >= 1
                pa, pz = BATCHES[(job + 2) % NB]
                lo, hi = pa * CHUNK, pz * CHUNK
                na, nz = BATCHES[(job - 1) % NB]
                nlo, nhi = na * CHUNK, nz * CHUNK
                if has_p:
                    pool.wait_ge(*t.next("k_scan"))
                    tt(LW[:, lo:hi], Z1[:, lo:hi], LW[:, lo:hi], ALU.subtract, "k_excl")
                    pool.wait_ge(*t.next("k_ez2"))
                    for h in range(HEADS):
                        tt(AR[HALF[h], pa:pz, 1, h, :], chunks(RR[HALF[h], lo:hi]), Z2[HALF[h], pa:pz, :], ALU.mult, "k_arr")
                if has_n:
                    pool.wait_ge(*t.next("k_grs"))
                    tt(flat(Y)[:, nlo:nhi], flat(Y)[:, nlo:nhi], Q1[:, nlo:nhi], ALU.mult, "k_pn")
                if has_p:
                    pool.wait_ge(*t.next("k_ez1"))
                    pool.wait_ge(*t.next("k_k2"))
                    tt(BK[:, pa:pz, 1, :], chunks(KK[:, lo:hi]), chunks(Z1[:, lo:hi]), ALU.mult, "k_bk1")
                    pool.wait_ge(*t.next("k_kn"))
                    tt(X2[:, lo:hi], X1[:, lo:hi], AA[:, lo:hi], ALU.mult, "k_b")
                    tt(BK[:, pa:pz, 0, :], chunks(X2[:, lo:hi]), chunks(Z1[:, lo:hi]), ALU.mult, "k_bk")
                if has_n:
                    pool.wait_ge(*t.next("k_pt"))
                    tt(flat(Y)[:, nlo:nhi], flat(Y)[:, nlo:nhi], BON[:, nlo:nhi], ALU.add, "k_padd")
                    b = (job - 1) % NB
                    pool.wait_ge(*t.next(f"dma_pq{b}", 3 if b == NB - 1 else 2))
                    tt(GG[:, nlo:nhi], flat(Y)[:, nlo:nhi], GG[:, nlo:nhi], ALU.mult, "k_out")

            for job in (-2, -1, 0):
                interval(job)
            with pool.Fori(0, KT - 1) as turn:
                t.enter(turn, HEAD_TURN)
                t.latest, t.n["k_out"] = "k_bk", t.n.get("k_out", 0)
                for job in (1, 2, 3):
                    interval(job, turn)
                t.leave(KT - 1)
            for job in (JOBS - 2, JOBS - 1, JOBS):
                interval(job)
            t.latest = None
            w_lo()
            for k in range(KT):
                if k == 4:
                    w_lo()
                h_lo(k)
            w_lo(KT)
            for k in range(KT):
                h_lo(k)
            ffn()

        @block.tensor
        def _(pe):
            t = Tally(pe, sems)

            def split_product(m, blocks, last=None):
                acc = ACC[m % 2]
                if m >= 2:
                    pe.wait_ge(*t.at(f"taken{m % 2}", m // 2))
                for i, (wh, wl, xh, xl, before, after) in enumerate(blocks):
                    if before:
                        before()
                    for q, (a, b) in enumerate(((wh, xh), (wh, xl), (wl, xh))):
                        for j in range(CH):
                            mm = pe.matmul(acc[:, j, :], a, b[:, j * CW:(j + 1) * CW],
                                           start=(i == 0 and q == 0), stop=(i == len(blocks) - 1 and q == 2))
                    if after:
                        mm.then_inc(*t.made(after))
                mm.then_inc(*t.made("acc_ready"))

            def up(m, n, fresh=False, release=False):
                s = n % 2
                pe.wait_ge(*t.next("w_lo"))
                split_product(m, [(WH[s][:, k, :], WL[s][:, k, :], HH[:, k, :], HL[:, k, :],
                                   (lambda k=k: pe.wait_ge(*t.next("h_lo1" if k % 2 else "h_lo"))) if fresh else None,
                                   "h_used" if release and k < KT - 1 else None) for k in range(KT)])

            def down(m, n, s):
                pe.wait_ge(*t.next("p_lo", 2))
                for d in range(KT):
                    if d % 4 == 0:
                        pe.wait_ge(*t.next("w_lo"))
                    w = (n + d // 4) % 2
                    split_product(m + d, [(WH[w][:, 2 * (d % 4) + k, :], WL[w][:, 2 * (d % 4) + k, :],
                                           PH[:, 2 * (s % 2) + k, :], PL[:, 2 * (s % 2) + k, :], None, None)
                                          for k in range(2)])
                return m + KT, n + 2

            def norm(m):
                pe.wait_ge(*t.next("summed", KT - 1))
                if m >= 2:
                    pe.wait_ge(*t.at(f"taken{m % 2}", m // 2))
                for j in range(CH):
                    mm = pe.matmul(ACC[m % 2][:, j, :], ONES, T[:, 3, j * CW:(j + 1) * CW], start=True, stop=True)
                mm.then_inc(*t.made("acc_ready"))

            pe.wait_ge(*t.at("dma_const", 2))
            norm(0)
            m, n = M_LRU, 0

            def gates(m, f):
                pe.wait_ge(*t.next("conv"))
                pe.wait_ge(*t.next(f"dma_gw{f % 2}"))
                for q in range(2):
                    if m + q >= 2:
                        pe.wait_ge(*t.at(f"taken{(m + q) % 2}", (m + q) // 2))
                    for j in range(CH):
                        mm = pe.matmul(ACC[(m + q) % 2][:, j, :], GW[f % 2][:, q, :], T[:, 1, j * CW:(j + 1) * CW],
                                       start=True, stop=True)
                    mm.then_inc(*t.made("acc_ready"))

            for g in range(LRU_GROUPS):
                for q in range(3):
                    up(m + q, n + q, fresh=(g == 0 and q == 0))
                gates(m + 3, 2 * g)
                up(m + 5, n + 3)
                m, n = m + 6, n + 4
                if g:
                    m, n = down(m, n, g - 1)
                gates(m, 2 * g + 1)
                m += 2
            m, n = down(m, n, LRU_GROUPS - 1)
            norm(m)
            m += 1

            def ffn(m, n):
                def step(m, n, fresh=False):
                    for q in range(4):
                        up(m + q, n + q, fresh=fresh and q == 0)
                    return m + 4, n + 4

                m, n = step(m, n, fresh=True)
                with pe.Fori(0, FFN_TURNS) as turn:
                    t.enter(turn, FFN_TURN)
                    a, b = m, n
                    for s in (1, 2):
                        a, b = step(a, b)
                        a, b = down(a, b, s - 1)
                    t.leave(FFN_TURNS)
                m, n = m + 24 * FFN_TURNS, n + 12 * FFN_TURNS
                m, n = step(m, n)
                m, n = down(m, n, STEPS - 2)
                return down(m, n, STEPS - 1)

            m, n = ffn(m, n)
            norm(m)
            m += 1
            for q in range(3):
                up(m + q, n + q, fresh=True, release=True)
            m, n = m + 3, n + 3
            for j in range(3):
                pe.wait_ge(*t.next("w_lo"))
                pe.wait_ge(*t.at("lora_lo", 2 if j == 2 else 1))
                s, r = n % 2, 2 if j == 2 else 0
                for f in range(KT):
                    split_product(m, [(WH[s][:, f, :], WL[s][:, f, :], TR[:, r, 0:COLS], TR[:, r + 1, 0:COLS], None, None)])
                    m += 1
                n += 1
            with pe.Fori(0, 3) as turn:
                t.enter(turn, dict(w_lo=KT, h_lo=KT // 2, h_lo1=KT // 2, acc_ready=KT, taken0=KT // 2, taken1=KT // 2, h_used=KT - 1))
                for f in range(KT):
                    up(m + f, n + f, fresh=(f == 0), release=(f == KT - 1))
                t.leave(3)
            m, n = m + 3 * KT, n + 3 * KT
            assert (m, n) == (M_OUT, W_OUT)

            pe.wait_ge(*t.at("zeroed", 6))
            pe.wait_ge(*t.at("dma_const2", 3))
            pe.wait_ge(*t.at("taken0", (M_OUT + 1) // 2))
            pe.wait_ge(*t.at("taken1", M_OUT // 2))

            def interval(job, turn=None):
                has_s, has_l, has_p, has_n = 0 <= job < JOBS, 0 <= job + 1 < JOBS, job + 2 < JOBS, job >= 1
                f, b = divmod(job, NB)
                a, z = BATCHES[b]
                la, lz = BATCHES[(job + 1) % NB]
                pb = (job + 2) % NB
                pa, pz = BATCHES[pb]
                na, nz = BATCHES[(job - 1) % NB]
                q = job + 2
                inv = job + 1

                def sums(bank, src, event):
                    pe.matmul(PS[:, bank, 0:src.shape[-1]], BD, src, start=True, stop=True).then_inc(*t.made(event))

                def products(g):
                    ga, gz = groups(pb, 2)[g]
                    bank = 4 + g % 2
                    if g == 0:
                        pe.wait_ge(*t.next("k_bkt", 2))
                        pe.wait_ge(*t.next("k_ar", 2))
                        pe.wait_ge(*t.next("k_arr", 2))
                    elif g == 2:
                        pe.wait_ge(*t.at("k_gm", 3 * q + 1))
                    for c in range(ga, gz):
                        for h in range(HEADS):
                            col = ((c - ga) * HEADS + h) * P
                            mm = pe.matmul(PS[:, bank, col:col + P].rearrange("p (s c) -> p s c", s=2),
                                           BK[:, c, :, :].rearrange("p s c -> p (s c)"), AR[:, c, :, h, :],
                                           start=True, stop=True)
                    mm.then_inc(*t.made("k_g"))

                def turn_inverse(k):
                    pe.wait_ge(*t.at("k_ms", LEVELS * inv + k + 1))
                    if job >= 0 or k:
                        pe.wait_ge(*t.at("k_nd", 4 * (LEVELS * inv + k)))
                    for i, c in enumerate(range(la, lz, 2)):
                        mm = pe.transpose(PS[:, 7, i * P:(i + 1) * P], MS[:, c:c + 2, :].rearrange("p n c -> p (n c)"), ID)
                    mm.then_inc(*t.made("k_mt"))

                for k in range(LEVELS):
                    c = a + k if has_s and a + k < z else None
                    if c is not None:
                        if c == a:
                            pe.wait_ge(*t.at("k_gm", 3 * (job + 1)))
                        if job or k:
                            pe.wait_ge(*t.next("k_s"))
                        first = c == 0
                        S = SIN if c == NCH - 1 else SS[(c - 1) % 2]
                        if c == NCH - 1:
                            pe.wait_ge(*t.next("dma_sin"))
                        for h in range(HEADS):
                            mm = pe.matmul(PS[HALF[h], 0, 0:CHUNK], G[:, c, h, 0:CHUNK], UV[:, c, h, :],
                                           start=True, stop=first, skip_group_check=True)
                        if not first:
                            mm = pe.matmul(PS[:, 0, 0:CHUNK], AR[:, c, 0, :, :].rearrange("p h c -> p (h c)"), S[:, :],
                                           start=False, stop=True, skip_group_check=True)
                        mm.then_inc(*t.made("k_rhs"))
                    if has_l:
                        if k:
                            turn_inverse(k - 1)
                        else:
                            pe.wait_ge(*t.next("k_lt", 6))
                            if job >= 0:
                                pe.wait_ge(*t.at("k_ms", LEVELS * inv))
                        for i in range(la, lz):
                            mm = pe.matmul(PS[:, 6, (i - la) * CHUNK:(i - la + 1) * CHUNK],
                                           LT[:, i, :, :].rearrange("p h c -> p (h c)"),
                                           MS[:, i, :] if k else IST[:, :], start=True, stop=True)
                        mm.then_inc(*t.made("k_a"))
                    if c is not None:
                        if c == a:
                            pe.wait_ge(*t.at("k_nd", 4 * LEVELS * (job + 1)))
                        pe.wait_ge(*t.next("k_rhss"))
                        pe.matmul(PS[:, 1, 0:CHUNK], ND[:, c, :, :].rearrange("p h c -> p (h c)"), RHS[:, :],
                                  start=True, stop=True, skip_group_check=True).then_inc(*t.made("k_sa"))
                    if k == 0 and has_p:
                        pe.wait_ge(*t.next("k_sq"))
                        if q:
                            pe.wait_ge(*t.at("k_bonus", q))
                        sums(2, X2[:, pa * CHUNK:pz * CHUNK], "s_kk")
                    if k == 0 and has_n:
                        f0, b0 = divmod(job, NB)
                        pe.wait_ge(*t.at("k_ys", NCH * f0 + BATCHES[b0][0]))
                        sums(3, flat(Y)[:, na * CHUNK:nz * CHUNK], "s_mean")
                    if k == 1 and has_n:
                        pe.wait_ge(*t.next("k_csq"))
                        sums(3, Q1[:, na * CHUNK:nz * CHUNK], "s_var")
                    if k == 2 and has_p:
                        if q:
                            pe.wait_ge(*t.at("k_gm", 3 * q))
                        for i, v in enumerate(range(pa, pz, 2)):
                            mm = pe.transpose(PS[:, 5, i * P:(i + 1) * P], VV[:, v * CHUNK:(v + 2) * CHUNK], ID)
                        mm.then_inc(*t.made("k_tv"))
                    if k == 3 and has_p:
                        pe.wait_ge(*t.next("k_prep"))
                        sums(2, X3[:, pa * CHUNK:pz * CHUNK], "s_bon")
                    if k >= 4 and has_p:
                        products(k - 4)
                    if c is not None:
                        pe.wait_ge(*t.next("k_uv", 2))
                        for h in range(HEADS):
                            mm = pe.matmul(PS[HALF[h], 0, 0:CHUNK], BKT[:, c, h * CHUNK:(h + 1) * CHUNK],
                                           UV[:, c, h, :], start=True, stop=True, skip_group_check=True)
                        mm.then_inc(*t.made("k_sp"))
                        for h in range(HEADS):
                            out = PS[HALF[h], 1, 0:CHUNK]
                            if not first:
                                pe.matmul(out, S[:, :], AR[:, c, 1, h, :], start=True, stop=False, skip_group_check=True)
                            mm = pe.matmul(out, UV[:, c, h, :], G[:, c, h, CHUNK:2 * CHUNK], start=first, stop=True,
                                           skip_group_check=True)
                        mm.then_inc(*t.made("k_y"))
                    if k == 3 and has_p:
                        pe.wait_ge(*t.next("k_bk"))
                        for g, (ga, gz) in enumerate(groups(pb, 3)):
                            if g:
                                pe.wait_ge(*t.next("k_vt", 2))
                            for i in range(ga, gz):
                                mm = pe.transpose(PS[:, 4 + g, (i - ga) * P:(i - ga + 1) * P],
                                                  BK[:, i, :, :].rearrange("p s c -> p (s c)"), ID)
                            mm.then_inc(*t.made("k_tb"))
                    if has_l and k:
                        pe.wait_ge(*t.at("k_am", LEVELS * inv + k + 1))
                        pe.wait_ge(*t.at("k_nd", 4 * (LEVELS * inv + k)))
                        for i in range(la, lz):
                            mm = pe.matmul(PS[:, 6, (i - la) * CHUNK:(i - la + 1) * CHUNK],
                                           ND[:, i, :, :].rearrange("p h c -> p (h c)"), AS[:, i, :], start=True, stop=True)
                        mm.then_inc(*t.made("k_mm"))
                if has_p:
                    products(2)
                if has_l:
                    turn_inverse(LEVELS - 1)

            for job in (-2, -1, 0):
                interval(job)
            with pe.Fori(0, KT - 1) as turn:
                t.enter(turn, HEAD_TURN)
                for job in (1, 2, 3):
                    interval(job, turn)
                t.leave(KT - 1)
            for job in (JOBS - 2, JOBS - 1, JOBS):
                interval(job)
            pe.wait_ge(*t.at("k_gln", JOBS))
            pe.wait_ge(*t.at("k_bonus", JOBS))
            pe.wait_ge(*t.at("k_s", KT * NCH))
            for f in range(KT):
                up(m, n, fresh=(f == 0))
                m, n = m + 1, n + 1
            norm(m)
            m += 1
            m, n = ffn(m, n)
            norm(m)
            assert (m, n) == (M_N4, N_TILES)

        @block.vector
        def _(dve):
            t = Tally(dve, sems)

            def tt(out, a, b, op, event, n=None):
                if t.latest:
                    dve.wait_ge(*t.own())
                dve.tensor_tensor(out, a, b, op).then_inc(*t.made(event, n))

            def ts(out, a, s1, s2, op1, op2, event):
                if t.latest:
                    dve.wait_ge(*t.own())
                dve.tensor_scalar(out, a, s1, s2, op1, op2).then_inc(*t.made(event))

            def stt(out, a, s, b, op1, op2, event, n=None):
                if t.latest:
                    dve.wait_ge(*t.own())
                dve.scalar_tensor_tensor(out=out, in0=a, scalar=s, in1=b, op0=op1, op1=op2).then_inc(*t.made(event, n))

            def copy(out, a, event):
                if t.latest:
                    dve.wait_ge(*t.own())
                dve.tensor_copy(out, a).then_inc(*t.made(event))

            def fill(out, value, event):
                if t.latest:
                    dve.wait_ge(*t.own())
                dve.memset(out, value).then_inc(*t.made(event))

            def add_squares(k):
                dve.wait_ge(*t.next("squared", 2 if k == 1 else 1))
                tt(T[:, 3, 0:COLS], T[:, 3, 0:COLS], T[:, 4 + k % 2, 0:COLS], ALU.add, "summed")

            def h_lo(q, row=None):
                dve.wait_ge(*t.at("h_hi", q + 1))
                k = q % KT
                tt(HL[:, k, :], T[:, 4 + k % 4 if row is None else row, 0:COLS], HH[:, k, :], ALU.subtract, "h_lo1")

            def h_rows(name, at, event="h_full"):
                dve.wait_ge(*t.next("rstd"))
                for k in range(KT):
                    if event == "hf":
                        out = HF[:, k, PAD:ROW]
                    elif name == "final":
                        out = T[:, 4 + k % 2, 0:COLS]
                        if k >= 2:
                            dve.wait_ge(*t.at(f"dma_y{k % 2}", k // 2))
                    else:
                        out = T[:, 4 + k % 4, 0:COLS]
                        if k >= 4 and k % 2 == 0:
                            dve.wait_ge(*t.at("h_lo", (at + k - 4) // 2 + 1))
                    stt(out, X[:, k, :], vec(name, k), T[:, 2, 0:COLS], ALU.mult, ALU.mult, event)
                    if event == "h_full" and name != "final" and k % 2 == 0 and k:
                        h_lo(at + k - 1)
                if event == "h_full" and name != "final":
                    h_lo(at + KT - 1)

            def conv(src, out, taps, bias, between=None):
                last = len(taps) - 1
                ts(out, src[:, PAD:ROW], taps[last], bias, ALU.mult, ALU.add, "tap")
                for j in range(last - 1, -1, -1):
                    if j == 0 and between is not None:
                        take(between, 0)
                    back = last - j
                    stt(out, src[:, PAD - back:ROW - back], taps[j], out, ALU.mult, ALU.add, "tap" if j else "conv")

            def take(m, d, bias=None):
                dve.wait_ge(*t.at("acc_ready", m + 1))
                x = row3(X[:, d, :])
                if bias is None:
                    tt(x, ACC[m % 2], x, ALU.add, f"taken{m % 2}", m // 2 + 1)
                else:
                    stt(x, ACC[m % 2], bias, x, ALU.add, ALU.add, f"taken{m % 2}", m // 2 + 1)

            def take_all(m, last, bias=False, first=0):
                for d in range(first, KT):
                    take(m + d, d, vec("b_out", d) if bias else None)
                    if last and d >= 2:
                        add_squares(d - 1)
                if last:
                    add_squares(KT - 1)

            dve.wait_ge(*t.at("dma_const", 2))
            fill(T[:, 0:2, 0:PAD], 0.0, "pads")
            ts(DV[:, 0:6, :].rearrange("p a b -> p (a b)"), V[:, VAT["mu0"]:VAT["mu0"] + 6 * KT], -1.0, 1.0, ALU.mult, ALU.add, "pads")
            dve.wait_ge(*t.next("absv", 3))
            E_, Z_, W_, A_ = DV[:, 6, :], DV[:, 9, :], DV[:, 10, :], DV[:, 11, :]
            ts(Z_, E_, 2.0, None, ALU.add, ALU.bypass, "pads")
            if t.latest:
                dve.wait_ge(*t.own())
            dve.reciprocal(Z_, Z_).then_inc(*t.made("pads"))
            tt(Z_, Z_, E_, ALU.mult, "pads")
            tt(W_, Z_, Z_, ALU.mult, "pads")
            ts(A_, W_, 1.0 / 15, None, ALU.mult, ALU.bypass, "pads")
            for c in (13, 11, 9, 7, 5, 3):
                stt(A_, A_, 1.0 / c, W_, ALU.add, ALU.mult, "pads")
            stt(A_, A_, 1.0, Z_, ALU.add, ALU.mult, "pads")
            stt(DV[:, 8, :], A_, 2.0, DV[:, 7, :], ALU.mult, ALU.add, "pads")
            ts(DV[:, 8, :], DV[:, 8, :], 4.0, None, ALU.mult, ALU.bypass, "vprep")
            for k in range(1, KT):
                add_squares(k)
            h_rows("mix0", 0)

            UB, U = T[:, 0, :], T[:, 1, 0:COLS]
            R, I, S, Q = (T[:, r, 0:COLS] for r in (4, 5, 6, 7))

            def lru_conv(m, f):
                dve.wait_ge(*t.at(f"taken{m % 2}", m // 2 + 1))
                for j in range(3):
                    copy(UB[:, PAD + HIST - 2 + j:PAD + HIST - 1 + j], vec(f"lc{j}", f), "hist")
                copy(ST[:, f, 0:6].rearrange("p (s c) -> p s c", s=2), tails(UB[:, PAD:], 3), "kept")
                conv(UB, U, [vec(f"cw{j}", f) for j in range(4)], vec("cb", f))

            def lru_scan(m, f):
                dve.wait_ge(*t.at(f"taken{(m + 1) % 2}", (m + 1) // 2 + 1))
                tt(I, I, U, ALU.mult, "post")
                dve.wait_ge(*t.next("tan"))
                ts(Q, R, 1.0, None, ALU.add, ALU.bypass, "post")
                if t.latest:
                    dve.wait_ge(*t.own())
                dve.reciprocal(Q, Q).then_inc(*t.made("post"))
                dve.wait_ge(*t.next("root"))
                ts(R, Q, 2.0, -1.0, ALU.mult, ALU.add, "post")
                tt(S, S, Q, ALU.mult, "post")
                tt(S, S, I, ALU.mult, "post")
                fill(R[:, HIST:SAMPLE], 0.0, "post")
                copy(S[:, HIST:SAMPLE], vec("h0", f), "post")
                if t.latest:
                    dve.wait_ge(*t.own())
                dve.tensor_tensor_scan(Q, R, S, 0.0, ALU.mult, ALU.add).then_inc(*t.made("post"))
                copy(ST[:, f, 6:8].rearrange("p (s c) -> p s c", s=2), tails(Q, 1), "kept")
                tt(S, Q, T[:, 2 + f % 2, 0:COLS], ALU.mult, "p_full")

            m = M_LRU
            for g in range(LRU_GROUPS):
                f = 2 * g
                lru_conv(m + 1, f)
                lru_scan(m + 3, f)
                lru_conv(m + 5, f + 1)
                m += 6
                if g:
                    take_all(m, False, bias=(g == 1))
                    m += KT
                lru_scan(m, f + 1)
                m += 2
            take_all(m, True)
            m += KT
            fill(T[:, 0:2, 0:PAD], 0.0, "pads")
            h_rows("ffn0", KT)
            m += 1

            def ffn(m, stored):
                def step(s, m):
                    b = s % 2
                    dve.wait_ge(*t.next(f"dma_fp{b}"))
                    if s or stored:
                        dve.wait_ge(*t.at(f"dma_fs{b}", stored + s // 2))
                    for j in range(2):
                        gate, val = T[:, 2 + 2 * j, 0:COLS], T[:, 3 + 2 * j, 0:COLS]
                        dve.wait_ge(*t.at("p_lo", t.n.get("p_full", 0) - 1))
                        for q, out in ((0, gate), (1, val)):
                            v = FP[b][:, 2 * j + q, :]
                            ub = T[:, q, :]
                            dve.wait_ge(*t.at(f"taken{m % 2}", m // 2 + 1))
                            copy(ub[:, PAD + HIST - 1:PAD + SAMPLE], v[:, 4:6], "hist")
                            copy(FS[b][:, 2 * j + q, :, :], tails(ub[:, PAD:], 2), "kept")
                            conv(ub, out, [v[:, c:c + 1] for c in range(3)], v[:, 3:4],
                                 m + 1 if s and j and q else None)
                            m += 1
                        if s and j:
                            take(m + 1, 1)
                        dve.wait_ge(*t.next("gelu"))
                        tt(gate, gate, val, ALU.mult, "p_full")
                    return m

                m = step(0, m)
                with dve.Fori(0, FFN_TURNS) as turn:
                    if t.latest:
                        dve.wait_ge(*t.own())
                    t.enter(turn, FFN_TURN)
                    a = m
                    for s in (1, 2):
                        a = step(s, a)
                        take_all(a, False, first=2)
                        a += KT
                    t.leave(FFN_TURNS)
                m += 24 * FFN_TURNS
                m = step(STEPS - 1, m)
                take_all(m, False, first=2)
                m += KT
                take_all(m, True)
                return m + KT

            m = ffn(m, 0)
            h_rows("mix1", 0, "hf")
            fill(HF[:, :, PAD - 1:PAD], 0.0, "hf")
            copy(HF[:, :, PAD + HIST:PAD + SAMPLE], V[:, VAT["shift"]:VAT["shift"] + KT].rearrange("p (k c) -> p k c", c=1), "hf")
            w = COLS - SEQ
            copy(ST[:, :, 8:10], HF[:, :, PAD + SEQ - w:ROW].rearrange("p k (s c) -> p k s c", s=2)[:, :, :, w - 1], "hf")
            for q, (j, k) in enumerate(((j, k) for j in MIXES for k in range(KT)), 2 * KT):
                dve.wait_ge(*t.next("mixhalf"))
                tmp = T[:, mix_row(q - 2 * KT), 0:COLS]
                stt(tmp, HF[:, k, PAD - 1:ROW - 1], vec(f"mu{j}", k), tmp, ALU.mult, ALU.add, "h_full")
                i = q - 2 * KT
                if i < 4 * KT:
                    odd = [i - 1] if i and k % 2 == 0 else []
                    if i == 4 * KT - 1:
                        odd = [i]
                else:
                    odd = {5: [i - 4], 6: [i - 3], 7: [i - 2, i]}.get(k, [])
                for o in odd:
                    h_lo(2 * KT + o, mix_row(o))

            dve.wait_ge(*t.at("zeroed", 6))
            dve.wait_ge(*t.at("dma_const2", 3))

            def interval(job, turn=None):
                has_s, has_l, has_p, has_n = 0 <= job < JOBS, 0 <= job + 1 < JOBS, job + 2 < JOBS, job >= 1
                f, b = divmod(job, NB)
                a, z = BATCHES[b]
                la, lz = BATCHES[(job + 1) % NB]
                pb = (job + 2) % NB
                pa, pz = BATCHES[pb]
                lo, hi = pa * CHUNK, pz * CHUNK
                na, nz = BATCHES[(job - 1) % NB]
                ncols = slice(na * CHUNK, nz * CHUNK)
                level_psum = PS[:, 6, 0:(lz - la) * CHUNK].rearrange("p (n c) -> p n c", c=CHUNK)

                def masked(g):
                    ga, gz = groups(pb, 2)[g]
                    dve.wait_ge(*t.next("k_g"))
                    n = (gz - ga) * HEADS
                    raw = PS[:, 4 + g % 2, 0:n * P].rearrange("p (n c) -> p n c", c=P)
                    for h in range(HEADS):
                        tt(LT[HALF[h], ga:gz, h, :], raw[HALF[0], h:n:HEADS, 0:CHUNK],
                           ML[HALF[0]].unsqueeze(1).to_broadcast([CHUNK, gz - ga, CHUNK]), ALU.mult, "k_lt")
                    tt(G[:, ga:gz, :, :].rearrange("p n h c -> p (n h) c"), raw,
                       MG.unsqueeze(1).to_broadcast([P, n, P]), ALU.mult, "k_gm")

                for k in range(LEVELS):
                    c = a + k if has_s and a + k < z else None
                    if c:
                        S = SIN if c == NCH - 1 else SS[(c - 1) % 2]
                        if c == NCH - 1:
                            dve.wait_ge(*t.next("dma_sin"))
                        ts(SPC[:, :], S[:, :], Z2[:, c, CHUNK - 1:CHUNK], None, ALU.mult, ALU.bypass, "k_scale")
                    if has_p and k == 0:
                        dve.wait_ge(*t.next(f"dma_in{pb}", 11 if pb == NB - 1 else 6))
                        if t.latest:
                            dve.wait_ge(*t.own())
                        dve.tensor_tensor_scan(Z1[:, lo:hi], SCAN[:, 0:hi - lo], LW[:, lo:hi], 0.0,
                                               ALU.mult, ALU.add).then_inc(*t.made("k_scan"))
                    if has_p and k == 1:
                        ts(X3[:, lo:hi], AA[:, lo:hi], -1.0, PP[pb][:, 1:2], ALU.add, ALU.mult, "k_ka")
                    if has_p and k == 2:
                        stt(X3[:, lo:hi], RR[:, lo:hi], PP[pb][:, 2:3], KK[:, lo:hi], ALU.mult, ALU.mult, "k_prep")
                    if has_n and k == 3:
                        dve.wait_ge(*t.next("k_pn"))
                        nb = (job - 1) % NB
                        dve.wait_ge(*t.next(f"dma_pq{nb}", 3 if nb == NB - 1 else 2))
                        ts(flat(Y)[:, ncols], flat(Y)[:, ncols], PQ[nb][:, 0:1], PQ[nb][:, 1:2], ALU.mult, ALU.add, "k_pt")
                    if c is not None:
                        dve.wait_ge(*t.next("k_sa"))
                        copy(UV[HALF[0], c, 0, :], PS[HALF[0], 1, 0:CHUNK], "k_uv")
                        copy(UV[HALF[0], c, 1, :], PS[HALF[1], 1, 0:CHUNK], "k_uv")
                    if has_l:
                        dve.wait_ge(*t.next("k_a"))
                        tt(AS[:, la:lz, :], level_psum, LV[:, k, :].unsqueeze(1).to_broadcast([P, lz - la, CHUNK]),
                           ALU.mult, "k_am")
                        if k == 0:
                            tt(MS[:, la:lz, :], AS[:, la:lz, :], IST[:, :].unsqueeze(1).to_broadcast([P, lz - la, CHUNK]),
                               ALU.add, "k_ms")
                    if c is not None:
                        dve.wait_ge(*t.next("k_sp"))
                        new, pc = PS[:, 0, 0:CHUNK], Z2[:, c, CHUNK - 1:CHUNK]
                        ends = c >= NCH - 2
                        out = SE[c - NCH + 2] if ends else SS[c % 2]
                        if c == NCH - 2:
                            if turn is not None or f:
                                dve.wait_ge(*t.at("dma_state", 2 * f))
                        if c == 0:
                            ts(out[:, :], new, pc, None, ALU.mult, ALU.bypass, "k_s")
                        else:
                            stt(out[:, :], new, pc, SPC[:, :], ALU.mult, ALU.add, "k_s")
                    if has_p and k == 0:
                        dve.wait_ge(*t.next("s_kk"))
                        ts(X2[:, lo:hi], PS[:, 2, 0:hi - lo], 1e-24, None, ALU.max, ALU.bypass, "k_max")
                    if has_n and k == 0:
                        dve.wait_ge(*t.next("s_mean"))
                        w = (nz - na) * CHUNK
                        stt(flat(Y)[:, ncols], PS[:, 3, 0:w], -1.0 / CHUNK, flat(Y)[:, ncols], ALU.mult, ALU.add, "k_cent")
                    if has_p and k == 1:
                        dve.wait_ge(*t.next("k_kk"))
                        stt(KK[:, lo:hi], X3[:, lo:hi], 1.0, KK[:, lo:hi], ALU.add, ALU.mult, "k_k2")
                    if has_p and k == 3:
                        dve.wait_ge(*t.next("k_elw"))
                        for h in range(HEADS):
                            stt(AR[HALF[h], pa:pz, 0, h, :], chunks(X1[HALF[h], lo:hi]), -1.0, chunks(LW[HALF[h], lo:hi]),
                                ALU.mult, ALU.mult, "k_ar")
                    if has_p and k >= 4:
                        masked(k - 4)
                    if has_l and k:
                        dve.wait_ge(*t.next("k_mm"))
                        tt(MS[:, la:lz, :], level_psum, MS[:, la:lz, :], ALU.add, "k_ms")
                    if has_p and k == 2:
                        dve.wait_ge(*t.next("k_rn"))
                        tt(X1[:, lo:hi], X1[:, lo:hi], X2[:, lo:hi], ALU.mult, "k_kn")
                        dve.wait_ge(*t.next("k_tv"))
                        for i in range(2):
                            n = len(range(pa + i, pz, 2))
                            copy(UV[HALF[1], pa + i:pz:2, :, :],
                                 PS[HALF[i], 5, 0:n * P].rearrange("p (n h c) -> p n h c", h=HEADS, c=CHUNK), "k_vt")
                    if has_p and k == 3:
                        dve.wait_ge(*t.next("s_bon"))
                        if has_n:
                            dve.wait_ge(*t.next("k_padd"))
                        tt(BON[:, lo:hi], PS[:, 2, 0:hi - lo], VV[:, lo:hi], ALU.mult, "k_bonus")
                if has_p:
                    masked(2)

            for job in (-2, -1, 0):
                interval(job)
            with dve.Fori(0, KT - 1) as turn:
                t.enter(turn, HEAD_TURN)
                for job in (1, 2, 3):
                    interval(job, turn)
                t.leave(KT - 1)
            interval(JOBS - 2)
            dve.wait_ge(*t.at("k_bk", JOBS))
            fill(T[:, 4:8, SEQ:SAMPLE], 0.0, "m_clear")
            interval(JOBS - 1)
            interval(JOBS)
            fill(T[:, 0:2, 0:PAD], 0.0, "pads")
            for k in range(1, KT, 2):
                h_lo(8 * KT + k)
            for b in range(NB):
                dve.wait_ge(*t.at(f"dma_m{b}", KT))
            m = M_OUT
            take_all(m, True)
            m += KT
            h_rows("ffn1", 9 * KT)
            m += 1
            m = ffn(m, FFN_TURNS + 1)
            h_rows("final", 0)


HEAD_TURN = dict(dma_in0=6, dma_in1=6, dma_in2=11, dma_pq0=2, dma_pq1=2, dma_pq2=3, dma_sin=1, dma_m0=1, dma_m1=1, dma_m2=1,
                 dma_state=2, k_arr=2 * NB, k_ar=2 * NB, k_tb=2 * NB, k_bkt=2 * NB, k_vt=2 * NB, k_g=3 * NB, k_gm=3 * NB,
                 k_lt=6 * NB, k_a=LEVELS * NB, k_am=LEVELS * NB, k_mm=(LEVELS - 1) * NB, k_ms=LEVELS * NB,
                 k_mt=LEVELS * NB, k_nd=4 * LEVELS * NB, k_rhs=NCH, k_rhss=NCH, k_sa=NCH, k_uv=2 * NCH, k_sp=NCH,
                 k_scale=NCH - 1, k_s=NCH, k_y=NCH, k_ys=NCH)
HEAD_TURN |= {name: NB for name in """k_kk k_sq s_kk k_max k_ln k_rn k_scan k_excl k_ez2 k_elw k_ez1 k_ka k_k2 k_prep k_kn
              k_b k_bk1 k_bk s_bon k_bonus k_tv s_mean k_cent k_csq s_var k_gln k_grs k_pn k_pt k_padd k_out""".split()}

INPUTS = dict(weights=(N_TILES, P, D), vectors=(P, NV), consts=(P, C_END), xT=(KT, P, COLS), gates=(KT, P, 2, P),
              ffn_vec=(2, STEPS, P, 4, 6), pair_vec=(2, KT, P, 4), wkv=(KT, P, CHUNK))
OUTPUTS = dict(yT=(KT, P, COLS), small=(P, KT, 10), ffn_state=(2, STEPS, P, 4, 2, 2), wkv_out=(2, KT, P, CHUNK))


def blocks(w, rows, cols):
    return np.stack([w[r * P:(r + 1) * P, c * P:(c + 1) * P] for r, c in zip(rows, cols)], 1)


def up_tile(w, f):
    return blocks(w, range(KT), [f] * KT)


def down_tiles(w, g):
    return [blocks(w, [2 * g + k for _ in range(4) for k in range(2)], [4 * t + d for d in range(4) for _ in range(2)])
            for t in range(2)]


def constants():
    r = np.arange(P)
    s, half = r % CHUNK, r // CHUNK
    c = np.zeros((P, C_END), np.float32)
    c[:, C_ONES:C_ONES + P] = 1
    c[:, C_BD:C_BD + P] = half[:, None] == half[None, :]
    c[:, C_ID:C_ID + P] = np.eye(P)
    upto, before = s[:, None] <= s[None, :], s[:, None] < s[None, :]
    is_a, is_k = half[None, :] == 0, half[:, None] == 1
    c[:, C_MG:C_MG + P] = np.where(is_a, before & is_k, upto)
    q = np.arange(CHUNK)
    c[:, C_ML:C_ML + CHUNK] = s[:, None] < q[None, :]
    for level in range(LEVELS):
        n = 1 << level
        same = s[:, None] // (2 * n) == q[None, :] // (2 * n)
        c[:, C_LV + level * CHUNK:C_LV + (level + 1) * CHUNK] = same & (s[:, None] & n != 0) & (q[None, :] & n == 0)
    c[:, C_IST:C_IST + CHUNK] = s[:, None] == q[None, :]
    c[:, C_SCAN:] = np.arange(BW)[None, :] % CHUNK != 0
    return c


def layout(a):
    f = lambda name: np.asarray(a[name])
    up, dn = f("ffn_w_up"), f("ffn_w_down")
    tiles = []
    wy, wx, wo = f("lru_w_y")[0], f("lru_w_x")[0], f("lru_w_out")[0]
    for g in range(LRU_GROUPS + 1):
        if g < LRU_GROUPS:
            tiles += [up_tile(wy, 2 * g), up_tile(wx, 2 * g), up_tile(wy, 2 * g + 1), up_tile(wx, 2 * g + 1)]
        if g:
            tiles += down_tiles(wo, g - 1)

    def ffn(layer):
        out = []
        for s in range(STEPS + 1):
            if s < STEPS:
                for q in (2 * s, FT + 2 * s, 2 * s + 1, FT + 2 * s + 1):
                    out.append(up_tile(up[layer], q))
            if s:
                out += down_tiles(dn[layer], s - 1)
        return out

    tiles += ffn(0)
    lora = np.concatenate([f("rw_w1")[0], f("rw_a1")[0]], 1)
    z = np.zeros((CHUNK, D), lora.dtype)
    tiles += [up_tile(lora, 0), up_tile(lora, 0), up_tile(f("rw_g1")[0], 0)]
    for w in (np.concatenate([f("rw_w2")[0], z]), np.concatenate([z, f("rw_a2")[0]]), f("rw_g2")[0]):
        tiles.append(blocks(w, [0] * KT, range(KT)))
    for name in ("rw_w_r", "rw_w_k", "rw_w_v", "rw_w_o"):
        tiles += [up_tile(f(name)[0], q) for q in range(KT)]
    tiles += ffn(1)
    weights = np.stack(tiles).reshape(N_TILES, P, D)

    col = lambda v: np.asarray(v).reshape(KT, P).T
    conv, mu = f("lru_conv_w")[0], f("rw_mu")[0]
    vecs = dict(mix0=f("norm_mix")[0], mix1=f("norm_mix")[1], ffn0=f("norm_ffn")[0], ffn1=f("norm_ffn")[1],
                final=f("norm_final"), b_x=f("lru_b_x")[0], b_y=f("lru_b_y")[0], cb=f("lru_conv_b")[0],
                ga_b=f("lru_ga_b")[0], gx_b=f("lru_gx_b")[0], lam=f("lru_lambda")[0], b_out=f("lru_b_out")[0],
                h0=f("state_lru_h")[0, 0], shift=f("state_rwkv_shift")[0, 0], w0=f("rw_w0")[0], a0=f("rw_a0")[0])
    vecs |= {f"cw{j}": conv[j] for j in range(4)} | {f"lc{j}": f("state_lru_conv")[0, 0, j] for j in range(3)}
    vecs |= {f"mu{j}": mu[j] for j in range(6)}
    vectors = np.concatenate([col(vecs[name]) for name in VEC], 1)

    xT = np.zeros((D, COLS), np.float32)
    xT[:, :SEQ] = f("x_prompt")[0].T
    xT[:, SAMPLE:] = f("x_sample")[0].T
    gates = np.stack([f("lru_ga_w")[0], f("lru_gx_w")[0]], 2)
    v = np.concatenate([f("ffn_conv_w"), f("ffn_conv_b")[:, None], f("state_ffn_conv")[:, 0]], 1)
    v = v.reshape(2, 6, 2, STEPS, 2, P).transpose(0, 3, 5, 4, 2, 1).reshape(2, STEPS, P, 4, 6)
    zero = np.zeros(D, np.float32)
    pair = np.stack([np.stack([w.reshape(KT, P) for w in ws], -1) for ws in (
        (f("rw_k_k")[0], f("rw_k_a")[0], f("rw_r_k")[0].reshape(-1), zero), (f("rw_ln_w")[0], f("rw_ln_b")[0], zero, zero))])
    wkv = f("state_rwkv_wkv")[0, 0].transpose(0, 2, 1).reshape(KT, P, CHUNK)
    return dict(weights=weights, vectors=vectors, consts=constants(), xT=xT.reshape(KT, P, COLS), gates=gates,
                ffn_vec=v, pair_vec=pair, wkv=wkv)


def outputs(r):
    y = r["yT"].reshape(D, COLS).T
    small = r["small"].transpose(2, 1, 0).reshape(10, D)
    fs = r["ffn_state"].reshape(2, STEPS, P, 2, 2, 2, 2).transpose(5, 0, 6, 4, 1, 3, 2).reshape(2, 2, 1, 2, 2 * FF)
    wkv = r["wkv_out"].reshape(2, 1, 1, KT * HEADS, CHUNK, CHUNK).transpose(0, 1, 2, 3, 5, 4)
    streams = [(small[None, None, 3 * s:3 * s + 3], small[None, 6 + s:7 + s], small[None, 8 + s:9 + s], wkv[s], fs[s])
               for s in range(2)]
    out = (y[None, :SEQ], y[None, SAMPLE:]) + streams[0] + streams[1]
    return tuple(np.ascontiguousarray(x) for x in out)


def kernel(**inputs):
    import concourse.bacc as bacc
    from concourse.bass_utils import run_bass_kernel_spmd

    arrays = {k: np.ascontiguousarray(v) for k, v in layout(inputs).items()}
    nc = bacc.Bacc("TRN2", target_bir_lowering=False, num_devices=1)
    io = {k: nc.dram_tensor(k, list(s), F32, kind="ExternalInput").ap() for k, s in INPUTS.items()}
    io |= {k: nc.dram_tensor(k, list(s), F32, kind="ExternalOutput").ap() for k, s in OUTPUTS.items()}
    io["scratch"] = nc.dram_tensor("scratch", [6, KT, P, COLS], F32, kind="Internal").ap()
    io["scratch_m"] = nc.dram_tensor("scratch_m", [KT, P, PACK], F32, kind="Internal").ap()
    build(nc, io)
    return outputs(run_bass_kernel_spmd(nc, [arrays], core_ids=[0]).results[0])
```
